# Optimizing a Trainium2 kernel written in Bass

```python
import jax, jax.numpy as jnp
from jax import lax
import numpy as np

D_MODEL = 1024
BATCH = 1
SEQ = 256
DEPTH = 2

MIX_WIDTH = D_MODEL // 4
HEAD_DIM = 64
N_BRANCH = 4

A_WIDTH = MIX_WIDTH
A_GROUPS = A_WIDTH // HEAD_DIM
A_GROUP_DIM = A_WIDTH // A_GROUPS
A_CHUNK = 128

B_HEADS = MIX_WIDTH // HEAD_DIM
B_HEAD_DIM = HEAD_DIM
B_ROT_DIM = B_HEAD_DIM // 4
MOBA_BLOCK = 256
MOBA_TOPK = 3
MOBA_QBLK = 32

C_WIDTH = MIX_WIDTH
CONV_WIDTH = 3

D_HEADS = MIX_WIDTH // HEAD_DIM
D_NOPE = 64
D_ROPE = 32
D_V = 64
D_Q_LORA = 192
D_KV_LORA = 128
MLA_QBLK = 128

D_FF = 4 * D_MODEL
ROPE_THETA = 500000.0
NORM_EPS = 1e-6

SPLIT_SIZES = (A_WIDTH, A_WIDTH,
               B_HEADS * B_HEAD_DIM, B_HEADS * B_HEAD_DIM, B_HEADS * B_HEAD_DIM,
               C_WIDTH, C_WIDTH, C_WIDTH,
               D_Q_LORA, D_KV_LORA, D_ROPE,
               N_BRANCH * D_MODEL)
IN_COLS = (2 * A_WIDTH + 3 * B_HEADS * B_HEAD_DIM + 3 * C_WIDTH
           + D_Q_LORA + D_KV_LORA + D_ROPE + N_BRANCH * D_MODEL)

kernel_name = 'hybrid_gated_parallel_sgu_moba_shortconv_mla'

F32 = jnp.float32

def rms_norm(x, g):
    xf = x.astype(F32)
    y = xf * lax.rsqrt(jnp.mean(xf * xf, axis=-1, keepdims=True) + NORM_EPS)
    return (y * g.astype(F32)).astype(x.dtype)

def layer_norm(x, g, b):
    xf = x.astype(F32)
    mu = jnp.mean(xf, axis=-1, keepdims=True)
    xc = xf - mu
    var = jnp.mean(xc * xc, axis=-1, keepdims=True)
    return (xc * lax.rsqrt(var + 1e-5) * g.astype(F32) + b.astype(F32)).astype(x.dtype)

def rope_tables(dim, seq):
    inv = 1.0 / (ROPE_THETA ** (jnp.arange(0, dim, 2, dtype=F32) / dim))
    ang = jnp.arange(seq, dtype=F32)[:, None] * inv[None, :]
    return jnp.cos(ang), jnp.sin(ang)

def apply_rope(x, cos, sin):
    half = x.shape[-1] // 2
    x1 = x[..., :half].astype(F32)
    x2 = x[..., half:].astype(F32)
    c = cos[:, None, :]
    s = sin[:, None, :]
    return jnp.concatenate([x1 * c - x2 * s, x2 * c + x1 * s], axis=-1).astype(x.dtype)

def partial_rope(x, cos, sin):
    return jnp.concatenate([apply_rope(x[..., :B_ROT_DIM], cos, sin), x[..., B_ROT_DIM:]], axis=-1)

def split_columns(proj):
    parts = []
    start = 0
    for n in SPLIT_SIZES:
        parts.append(proj[..., start:start + n])
        start += n
    return parts

def chunked_sgu(u, v, ln_g, ln_b, w_s, b_s):
    bsz, s_len, _ = v.shape
    v = layer_norm(v, ln_g, ln_b)
    vc = v.reshape(bsz, s_len // A_CHUNK, A_CHUNK, A_GROUPS, A_GROUP_DIM)
    causal = jnp.arange(A_CHUNK)[:, None] >= jnp.arange(A_CHUNK)[None, :]
    w = jnp.where(causal[None], w_s, jnp.zeros((), w_s.dtype))
    sv = jnp.einsum('gts,bcsgd->bctgd', w, vc) + b_s.T[None, None, :, :, None]
    return u * sv.reshape(bsz, s_len, A_WIDTH)

def moba_attention(q, k, v):
    bsz, s_len, n_h, dh = q.shape
    s_pad = -(-s_len // MOBA_BLOCK) * MOBA_BLOCK
    pad = ((0, 0), (0, s_pad - s_len), (0, 0), (0, 0))
    qh = q.transpose(0, 2, 1, 3)
    kh = jnp.pad(k, pad).transpose(0, 2, 1, 3)
    vh = jnp.pad(v, pad).transpose(0, 2, 1, 3)
    nb = s_pad // MOBA_BLOCK
    n_cand = max(nb, MOBA_TOPK)
    kblk = kh.reshape(bsz, n_h, nb, MOBA_BLOCK, dh)
    vblk = vh.reshape(bsz, n_h, nb, MOBA_BLOCK, dh)
    kmean = jnp.mean(kblk.astype(F32), axis=3)
    scale = dh ** -0.5
    gather = jax.vmap(jax.vmap(lambda blocks, idx: blocks[idx]))
    kl = MOBA_TOPK * MOBA_BLOCK

    def step(i):
        q0 = i * MOBA_QBLK
        qb = lax.dynamic_slice_in_dim(qh, q0, MOBA_QBLK, axis=2)
        cur = q0 // MOBA_BLOCK
        gate = jnp.einsum('bhqd,bhnd->bhqn', qb.astype(F32), kmean)
        if n_cand > nb:
            gate = jnp.pad(gate, ((0, 0), (0, 0), (0, 0), (0, n_cand - nb)))
        gate = jnp.where(jnp.arange(n_cand) < cur, gate, -jnp.inf)
        _, idx = lax.top_k(gate, MOBA_TOPK)
        idx = jnp.minimum(idx, nb - 1)
        valid = jnp.arange(MOBA_TOPK) < cur
        ksel = gather(kblk, idx)
        vsel = gather(vblk, idx)
        s_sel = jnp.einsum('bhqd,bhqkld->bhqkl', qb, ksel, preferred_element_type=F32) * scale
        s_sel = jnp.where(valid[:, None], s_sel, -jnp.inf).reshape(bsz, n_h, MOBA_QBLK, kl)
        kown = lax.dynamic_slice_in_dim(kh, cur * MOBA_BLOCK, MOBA_BLOCK, axis=2)
        vown = lax.dynamic_slice_in_dim(vh, cur * MOBA_BLOCK, MOBA_BLOCK, axis=2)
        s_own = jnp.einsum('bhqd,bhld->bhql', qb, kown, preferred_element_type=F32) * scale
        qpos = q0 + jnp.arange(MOBA_QBLK)
        kpos = cur * MOBA_BLOCK + jnp.arange(MOBA_BLOCK)
        s_own = jnp.where(kpos[None, :] <= qpos[:, None], s_own, -jnp.inf)
        p = jax.nn.softmax(jnp.concatenate([s_sel, s_own], axis=-1), axis=-1)
        p_sel = p[..., :kl].reshape(bsz, n_h, MOBA_QBLK, MOBA_TOPK, MOBA_BLOCK).astype(v.dtype)
        p_own = p[..., kl:].astype(v.dtype)
        return (jnp.einsum('bhqkl,bhqkld->bhqd', p_sel, vsel)
                + jnp.einsum('bhql,bhld->bhqd', p_own, vown))

    outs = lax.map(step, jnp.arange(s_len // MOBA_QBLK))
    return outs.transpose(1, 0, 3, 2, 4).reshape(bsz, s_len, n_h * dh)

def short_conv_mixer(bg, cg, xin, w_conv):
    z = cg * xin
    z = lax.conv_general_dilated(z, w_conv[:, None, :], window_strides=(1,),
                                 padding=[(CONV_WIDTH - 1, 0)],
                                 dimension_numbers=('NWC', 'WIO', 'NWC'),
                                 feature_group_count=C_WIDTH)
    return bg * z

def mla_attention(cq, ckv, kr, q_norm_g, w_uq, kv_norm_g, w_ukv, cos, sin):
    bsz, s_len, _ = cq.shape
    q = jnp.einsum('bsr,rhe->bshe', rms_norm(cq, q_norm_g), w_uq)
    q_nope = q[..., :D_NOPE]
    q_rope = apply_rope(q[..., D_NOPE:], cos, sin)
    kv = jnp.einsum('bsr,rhe->bshe', rms_norm(ckv, kv_norm_g), w_ukv)
    k_nope = kv[..., :D_NOPE]
    v = kv[..., D_NOPE:]
    k_rope = apply_rope(kr[:, :, None, :], cos, sin)[:, :, 0, :]
    scale = (D_NOPE + D_ROPE) ** -0.5
    kpos = jnp.arange(s_len)

    def step(i):
        q0 = i * MLA_QBLK
        qn = lax.dynamic_slice_in_dim(q_nope, q0, MLA_QBLK, axis=1)
        qr = lax.dynamic_slice_in_dim(q_rope, q0, MLA_QBLK, axis=1)
        s = (jnp.einsum('bqhn,bkhn->bhqk', qn, k_nope, preferred_element_type=F32)
             + jnp.einsum('bqhr,bkr->bhqk', qr, k_rope, preferred_element_type=F32)) * scale
        qpos = q0 + jnp.arange(MLA_QBLK)
        s = jnp.where(kpos[None, :] <= qpos[:, None], s, -jnp.inf)
        p = jax.nn.softmax(s, axis=-1).astype(v.dtype)
        return jnp.einsum('bhqk,bkhd->bqhd', p, v)

    outs = lax.map(step, jnp.arange(s_len // MLA_QBLK))
    return outs.transpose(1, 0, 2, 3, 4).reshape(bsz, s_len, D_HEADS * D_V)

def hybrid_layer(x, g_pre_mix, w_in, a_ln_g, a_ln_b, a_w_s, a_b_s, c_w_conv,
                 d_q_norm_g, d_w_uq, d_kv_norm_g, d_w_ukv, w_branch, w_out, g_post_mix,
                 g_pre_mlp, w_mlp_in, w_mlp_out, g_post_mlp, cos_b, sin_b, cos_d, sin_d):
    bsz, s_len, _ = x.shape
    h = rms_norm(x, g_pre_mix)
    (a_u, a_v, b_q, b_k, b_v, c_b, c_c, c_x,
     d_cq, d_ckv, d_kr, gate_logits) = split_columns(h @ w_in)

    out_a = chunked_sgu(jax.nn.gelu(a_u), jax.nn.gelu(a_v), a_ln_g, a_ln_b, a_w_s, a_b_s)
    hs = (bsz, s_len, B_HEADS, B_HEAD_DIM)
    out_b = moba_attention(partial_rope(b_q.reshape(hs), cos_b, sin_b),
                           partial_rope(b_k.reshape(hs), cos_b, sin_b),
                           b_v.reshape(hs))
    out_c = short_conv_mixer(c_b, c_c, c_x, c_w_conv)
    out_d = mla_attention(d_cq, d_ckv, d_kr, d_q_norm_g, d_w_uq, d_kv_norm_g, d_w_ukv, cos_d, sin_d)

    gates = jax.nn.sigmoid(gate_logits.reshape(bsz, s_len, N_BRANCH, D_MODEL))
    branches = (out_a, out_b, out_c, out_d)
    merged = gates[:, :, 0, :] * (branches[0] @ w_branch[0])
    for i in range(1, N_BRANCH):
        merged = merged + gates[:, :, i, :] * (branches[i] @ w_branch[i])
    x = x + rms_norm(merged @ w_out, g_post_mix)

    h = rms_norm(x, g_pre_mlp)
    y = jnp.square(jax.nn.relu(h @ w_mlp_in)) @ w_mlp_out
    return x + rms_norm(y, g_post_mlp)

def setup_inputs(seed: int = 0) -> dict:
    key = jax.random.key(seed)
    ks = jax.random.split(key, 20)
    L = DEPTH

    def nrm(k, shape, fan_in):
        return jax.random.normal(k, shape, F32) * (fan_in ** -0.5)

    def gain(k, shape):
        return 1.0 + 0.05 * jax.random.normal(k, shape, F32)

    return {
        'x': jax.random.normal(ks[0], (BATCH, SEQ, D_MODEL), F32),
        'g_pre_mix': gain(ks[1], (L, D_MODEL)),
        'w_in': nrm(ks[2], (L, D_MODEL, IN_COLS), D_MODEL),
        'a_ln_g': gain(ks[3], (L, A_WIDTH)),
        'a_ln_b': 0.02 * jax.random.normal(ks[4], (L, A_WIDTH), F32),
        'a_w_s': nrm(ks[5], (L, A_GROUPS, A_CHUNK, A_CHUNK), A_CHUNK),
        'a_b_s': gain(ks[6], (L, A_GROUPS, A_CHUNK)),
        'c_w_conv': nrm(ks[7], (L, CONV_WIDTH, C_WIDTH), CONV_WIDTH),
        'd_q_norm_g': gain(ks[8], (L, D_Q_LORA)),
        'd_w_uq': nrm(ks[9], (L, D_Q_LORA, D_HEADS, D_NOPE + D_ROPE), D_Q_LORA),
        'd_kv_norm_g': gain(ks[10], (L, D_KV_LORA)),
        'd_w_ukv': nrm(ks[11], (L, D_KV_LORA, D_HEADS, D_NOPE + D_V), D_KV_LORA),
        'w_branch': nrm(ks[12], (L, N_BRANCH, MIX_WIDTH, D_MODEL), MIX_WIDTH),
        'w_out': nrm(ks[13], (L, D_MODEL, D_MODEL), D_MODEL),
        'g_post_mix': gain(ks[14], (L, D_MODEL)),
        'g_pre_mlp': gain(ks[15], (L, D_MODEL)),
        'w_mlp_in': nrm(ks[16], (L, D_MODEL, D_FF), D_MODEL),
        'w_mlp_out': nrm(ks[17], (L, D_FF, D_MODEL), D_FF),
        'g_post_mlp': gain(ks[18], (L, D_MODEL)),
    }

def reference(x, g_pre_mix, w_in, a_ln_g, a_ln_b, a_w_s, a_b_s, c_w_conv,
              d_q_norm_g, d_w_uq, d_kv_norm_g, d_w_ukv, w_branch, w_out, g_post_mix,
              g_pre_mlp, w_mlp_in, w_mlp_out, g_post_mlp):
    s_len = x.shape[1]
    cos_b, sin_b = rope_tables(B_ROT_DIM, s_len)
    cos_d, sin_d = rope_tables(D_ROPE, s_len)
    for l in range(DEPTH):
        x = hybrid_layer(x, g_pre_mix[l], w_in[l], a_ln_g[l], a_ln_b[l], a_w_s[l], a_b_s[l],
                         c_w_conv[l], d_q_norm_g[l], d_w_uq[l], d_kv_norm_g[l], d_w_ukv[l],
                         w_branch[l], w_out[l], g_post_mix[l], g_pre_mlp[l], w_mlp_in[l],
                         w_mlp_out[l], g_post_mlp[l], cos_b, sin_b, cos_d, sin_d)
    return x


_drawn_inputs = setup_inputs


def setup_inputs(seed=0):
    import zlib

    import numpy as np

    out = dict(_drawn_inputs(seed))
    spreads = {}
    factors = {'a_ln_g': 3.367, 'a_ln_b': 8.0, 'd_q_norm_g': 8.0, 'd_kv_norm_g': 4.335, 'a_b_s': 2.882}
    for name, (base, spread) in spreads.items():
        noise = np.random.default_rng([zlib.crc32(name.encode()), seed]).standard_normal(out[name].shape)
        drawn = base * np.exp(spread * noise) if base else spread * noise
        out[name] = __import__('jax').numpy.asarray(drawn.astype(out[name].dtype))
    for name, factor in factors.items():
        out[name] = (out[name] * factor).astype(out[name].dtype)
    return out
```

```python
from contextlib import ExitStack

import concourse.bass as bass
from concourse import mybir

F32 = mybir.dt.float32
F32R = mybir.dt.float32r
ALU = mybir.AluOpType
ACT = mybir.ActivationFunctionType

P = 128
NORM_EPS = 1e-6
LN_EPS = 1e-5
GELU_CUBE = 0.044715
GELU_SCALE = 0.7978845608028654
B_ROT = 16
D_NOPE, D_ROPE, D_V = 64, 32, 64
Q_LORA, KV_LORA = 192, 128
MASKED = -3.0e38


def hybrid_trunk(nc: bass.Bass, x_in: bass.AP, g_pre_mix: bass.AP, w_in: bass.AP, a_ln_g: bass.AP,
                 a_ln_b: bass.AP, a_w_s: bass.AP, a_b_s: bass.AP, c_w_conv: bass.AP,
                 d_q_norm_g: bass.AP, d_w_uq: bass.AP, d_kv_norm_g: bass.AP, d_w_ukv: bass.AP,
                 w_branch: bass.AP, w_out: bass.AP, g_post_mix: bass.AP, g_pre_mlp: bass.AP,
                 w_mlp_in: bass.AP, w_mlp_out: bass.AP, g_post_mlp: bass.AP,
                 rope_tables: bass.AP, out: bass.AP):
    L, D, _ = w_in.shape
    S = x_in.shape[1]
    T = S // P
    KT = D // P
    MIX = w_branch.shape[2]
    FT = MIX // P
    NB = w_branch.shape[1]
    HEADS, HD = MIX // 64, 64
    FF = w_mlp_in.shape[2]
    A_GROUPS = a_w_s.shape[1]
    D_IN = Q_LORA + KV_LORA + D_ROPE
    QK = D_NOPE + D_ROPE
    assert (T, KT, FT, NB, HEADS, A_GROUPS) == (2, 8, 2, 4, 4, 4)

    COL_AV, COL_C, COL_D = MIX, 5 * MIX, 8 * MIX
    COL_GATE = COL_D + D_IN

    CHUNK = 2048
    FFC = CHUNK // KT
    STEPS = FF // FFC
    C_D, C_FEAT, C_GATE, C_BRANCH, C_OUT, C_MLP = 4, 8, 12, 28, 32, 36
    CHUNKS = C_MLP + 2 * STEPS
    GATE_STEPS = C_BRANCH - C_GATE
    RAW, RING = 2, 4
    assert CHUNKS % RING == 0 and STEPS % 2 == 0

    CONSTS = 8

    with ExitStack() as ctx:
        def sb(name, shape, dt=F32):
            return ctx.enter_context(nc.sbuf_tensor(name, shape, dt))[:]

        def sem(name):
            return ctx.enter_context(nc.semaphore(name))

        psum = ctx.enter_context(nc.psum_tensor("banks", [P, 8, 512], F32))[:]

        raw = sb("raw", [P, RAW, CHUNK])
        w_hi = sb("w_hi", [P, RING, CHUNK], F32R)
        w_lo = sb("w_lo", [P, RING, CHUNK], F32R)
        x = sb("x", [P, T, D])
        xT_hi = sb("xT_hi", [P, KT, S], F32R)
        xT_lo = sb("xT_lo", [P, KT, S], F32R)
        brT_hi = sb("brT_hi", [P, NB * FT, S], F32R)
        brT_lo = sb("brT_lo", [P, NB * FT, S], F32R)
        gain_pre = sb("gain_pre", [P, D])
        gain_post = sb("gain_post", [P, D])
        proj = sb("proj", [P, T, 4 * MIX])
        gated = proj.rearrange("p t (u n) -> p (t u) n", u=2)
        rows = sb("rows", [P, T * D])
        xn = rows.rearrange("p (t d) -> p t d", t=T)
        merged = rows.rearrange("p (u n) -> p u n", u=4)
        qD = rows[:, 0:T * HEADS * QK].rearrange("p (t h e) -> p t h e", t=T, h=HEADS)
        kD = rows[:, T * HEADS * QK:2 * T * HEADS * QK].rearrange("p (t h e) -> p t h e", t=T, h=HEADS)
        rope_tmp = rows[:, 2 * T * HEADS * QK:2 * T * HEADS * QK + 512].rearrange("p (a n) -> p a n", a=4)
        hidden_sq = rows[:, 0:512]
        hidden_relu = rows[:, 512:1536].rearrange("p (b n) -> p b n", b=2)
        gate_th = sb("gate_th", [P, NB * 2 * KT * P])
        gate_v = gate_th.rearrange("p (i j n) -> p i j n", i=NB, j=4)
        th1 = gate_th[:, 2048:4096]
        th2 = gate_th[:, 4096:6144]
        th3 = gate_th[:, 6144:8192]
        d_in = th1[:, 0:T * D_IN].rearrange("p (t n) -> p t n", t=T)
        w_uq = th1[:, 704:704 + 2 * HEADS * QK].rearrange("p (k n) -> p k n", k=2)
        w_ukv = th1[:, 1472:1472 + HEADS * (D_NOPE + D_V)]
        w_s = th2[:, 0:512].rearrange("p (g s) -> p g s", g=A_GROUPS)
        w_sT = th2[:, 512:1024].rearrange("p (g t) -> p g t", g=A_GROUPS)
        ln_g = th2[:, 1024:1280]
        ln_b = th2[:, 1280:1536]
        u2 = th2[:, 1536:2048]
        z = th3[:, 0:FT * (S + 2)].rearrange("p (f n) -> p f n", f=FT)
        conv = th3[:, 516:1028].rearrange("p (f n) -> p f n", f=FT)
        u_tmp = th3[:, 1028:1540]
        a_out = u_tmp
        av2 = sb("av2", [P, T, MIX])
        av_tmp = sb("av_tmp", [P, T, MIX])
        o_sb = av_tmp
        vD = sb("vD", [P, T, HEADS * D_V])
        qTB = sb("qTB", [P, FT, S])
        kTB = sb("kTB", [P, FT, S])
        qTD = sb("qTD", [P, HEADS, S])
        kTD = sb("kTD", [P, HEADS, S])
        cqT = qTD[:, 0:2, :]
        ckvT = qTD[:, 2, :]
        probs = sb("probs", [P, 2, 3 * P])
        probsT = sb("probsT", [P, 2, 3 * P])
        bias_s = sb("bias_s", [P, FT, P])
        vec_rows = sb("vec_rows", [9, P])
        vec_cols = sb("vec_cols", [P, 9])
        tables = sb("tables", [P, T, 2 * (B_ROT // 2 + D_ROPE // 2)])
        ident = sb("ident", [P, P])
        causal = sb("causal", [P, 2 * P])
        minus_half = sb("minus_half", [P, 4])
        norm_eps = sb("norm_eps", [P, 4])
        ln_eps = sb("ln_eps", [P, T])
        ss = sb("ss", [P, 4])
        ms = sb("ms", [P, 4])
        rstd = sb("rstd", [P, 4])
        ssD = sb("ssD", [P, 2, T])
        msD = sb("msD", [P, 2, T])
        rstdD = sb("rstdD", [P, 2, T])
        ln_stats = sb("ln_stats", [P, T, 6])
        ln_mv = sb("ln_mv", [P, T, 2])
        ln_ms = sb("ln_ms", [P, T])
        ln_rstd = sb("ln_rstd", [P, T])
        neg_max = sb("neg_max", [P, 2, T])
        row_sum = sb("row_sum", [P, 2, T, HEADS])
        inv_sum = sb("inv_sum", [P, 2, T, HEADS])
        start_mark = sb("start_mark", [P, 4])

        raw_landed = [sem(f"raw_landed{s}") for s in range(RAW)]
        hi_ready = sem("hi_ready")
        lo_ready = sem("lo_ready")
        chunk_used = sem("chunk_used")
        x_landed = sem("x_landed")
        tables_landed = sem("tables_landed")
        gain_pre_landed = sem("gain_pre_landed")
        gain_post_landed = sem("gain_post_landed")
        side_landed = sem("side_landed")
        consts_ready = sem("consts_ready")
        x_updated = sem("x_updated")
        x_added = sem("x_added")
        ss_ready = sem("ss_ready")
        ms_ready = sem("ms_ready")
        rstd_ready = sem("rstd_ready")
        xn_ready = sem("xn_ready")
        y_scaled = sem("y_scaled")
        xT_psum = sem("xT_psum")
        xT_hi_ready = sem("xT_hi_ready")
        xT_lo_ready = sem("xT_lo_ready")
        proj0_psum = sem("proj0_psum")
        proj_copied = sem("proj_copied")
        vec_psum = sem("vec_psum")
        ws_masked = sem("ws_masked")
        wsT_psum = sem("wsT_psum")
        vec_copied = sem("vec_copied")
        wsT_copied = sem("wsT_copied")
        ropeB_products = sem("ropeB_products")
        ropeB_ready = sem("ropeB_ready")
        qkTB_psum = sem("qkTB_psum")
        qkTB_copied = sem("qkTB_copied")
        av_squared = sem("av_squared")
        av_poly = sem("av_poly")
        av_inner = sem("av_inner")
        av_tanh = sem("av_tanh")
        av_gelu = sem("av_gelu")
        ln_stats_ready = sem("ln_stats_ready")
        ln_mv_ready = sem("ln_mv_ready")
        ln_ms_ready = sem("ln_ms_ready")
        ln_rstd_ready = sem("ln_rstd_ready")
        ln_centred = sem("ln_centred")
        ln_scaled = sem("ln_scaled")
        ln_ready = sem("ln_ready")
        d_in_copied = sem("d_in_copied")
        ssD_ready = sem("ssD_ready")
        msD_ready = sem("msD_ready")
        rstdD_ready = sem("rstdD_ready")
        d_normed = sem("d_normed")
        d_latentT_psum = sem("d_latentT_psum")
        d_latentT_copied = sem("d_latentT_copied")
        qD_psum = sem("qD_psum")
        kvD_psum = sem("kvD_psum")
        qkvD_copied = sem("qkvD_copied")
        ropeD_products = sem("ropeD_products")
        ropeD_ready = sem("ropeD_ready")
        qkTD_psum = sem("qkTD_psum")
        qkTD_copied = sem("qkTD_copied")
        z_ready = sem("z_ready")
        conv_tap = sem("conv_tap")
        c_out_ready = sem("c_out_ready")
        u_squared = sem("u_squared")
        u_poly = sem("u_poly")
        u_inner = sem("u_inner")
        u_tanh = sem("u_tanh")
        u_gelu = sem("u_gelu")
        sv_psum = sem("sv_psum")
        sv_biased = sem("sv_biased")
        a_out_ready = sem("a_out_ready")
        scores_psum = sem("scores_psum")
        scores_masked = sem("scores_masked")
        probs_ready = sem("probs_ready")
        probsT_psum = sem("probsT_psum")
        probsT_copied = sem("probsT_copied")
        attn_psum = sem("attn_psum")
        inv_sum_ready = sem("inv_sum_ready")
        attn_ready = sem("attn_ready")
        attnT_psum = sem("attnT_psum")
        brT_hi_ready = sem("brT_hi_ready")
        brT_lo_ready = sem("brT_lo_ready")
        gate_ready = sem("gate_ready")
        unit_psum = sem("unit_psum")
        unit_gated = sem("unit_gated")
        unit_added = sem("unit_added")
        mergedT_hi_ready = sem("mergedT_hi_ready")
        mergedT_lo_ready = sem("mergedT_lo_ready")
        y0_psum = sem("y0_psum")
        relu_ready = sem("relu_ready")
        hidden_squared = sem("hidden_squared")
        hidden_hi_ready = sem("hidden_hi_ready")
        hidden_lo_ready = sem("hidden_lo_ready")
        stored = sem("stored")
        wait_passed = sem("wait_passed")

        ORDER_C, ORDER_A, ORDER_B, ORDER_D = range(4)

        w_in_v = w_in.rearrange("l (k p) c -> l p k c", p=P)
        w_br_v = w_branch.rearrange("l i (k p) n -> l i p k n", p=P)
        w_out_v = w_out.rearrange("l (c k p) n -> l c p k n", p=P, k=2)
        mlp_in_v = w_mlp_in.rearrange("l (k p) (j c) -> l j p k c", p=P, c=FFC)
        mlp_out_v = w_mlp_out.rearrange("l (j k p) n -> l j p k n", p=P, k=FFC // P)
        PAIRS = STEPS // 2 - 1
        mlp_in_loop = w_mlp_in[:, :, 2 * FFC:].rearrange(
            "l (k p) (i b c) -> l i b p k c", p=P, b=2, c=FFC)
        mlp_out_loop = w_mlp_out[:, FFC:FF - FFC, :].rearrange(
            "l (i b k p) n -> l i b p k n", p=P, b=2, k=FFC // P)
        x_v = x_in.rearrange("a (t p) d -> t p (a d)", p=P)
        out_v = out.rearrange("a (t p) d -> t p (a d)", p=P)

        def shape_of(c):
            if c < C_D:
                return 4, 512
            if c < C_FEAT:
                return 2, D_IN
            if c < C_BRANCH:
                return KT, 256
            if c < C_MLP:
                return 2, D
            return (KT, FFC) if c == C_MLP or (c % 2 == 1 and c < C_MLP + 2 * STEPS - 1) else (2, D)

        def size_of(c):
            k, n = shape_of(c)
            return k * n

        def view(buf, c):
            k, n = shape_of(c)
            return buf[:, c % RING, 0:k * n].rearrange("p (k n) -> p k n", k=k)

        def both(c):
            return view(w_hi, c), view(w_lo, c)

        def nth(l, per_layer, i):
            return l * per_layer + i + 1

        def used(l, c):
            return nth(l, CHUNKS, c) + RING

        def split_done(l, c):
            return nth(l, CHUNKS, c) + RING

        def apart(eng):
            eng.sem_inc(wait_passed, 1)

        block = ctx.enter_context(nc.Block())

        @block.sync
        def _(sp):
            def load(l, c, src, i=0):
                sp.wait_ge(lo_ready, nth(l, CHUNKS, c + 4 * i) + RING - RAW)
                if c == C_GATE - 1:
                    apart(sp)
                k, n = shape_of(c)
                dst = raw[:, c % RAW, 0:k * n].rearrange("p (k n) -> p k n", k=k)
                sp.dma_start(dst, src).then_inc(raw_landed[c % RAW], 16)

            for t in range(T):
                sp.dma_start(x[:, t, :], x_v[t]).then_inc(x_landed, 16)
            with sp.Fori(0, L) as l:
                sp.dma_start(gain_pre, g_pre_mix[l].partition_broadcast(P)).then_inc(gain_pre_landed, 16)
                for c in range(C_D):
                    g, kh = c // 2, c % 2
                    col = COL_AV + 512 * g
                    load(l, c, w_in_v[l, :, 4 * kh:4 * kh + 4, col:col + 512])
                side = [
                    (vec_rows[0:6, :], c_w_conv[l].rearrange("k (f p) -> (k f) p", p=P)),
                    (vec_rows[6:7, :], d_q_norm_g[l, 0:P].unsqueeze(0)),
                    (vec_rows[7:8, 0:Q_LORA - P], d_q_norm_g[l, P:Q_LORA].unsqueeze(0)),
                    (vec_rows[8:9, :], d_kv_norm_g[l].unsqueeze(0)),
                    (w_s, a_w_s[l].rearrange("g t s -> t g s")),
                    (ln_g, a_ln_g[l].partition_broadcast(P)),
                    (ln_b, a_ln_b[l].partition_broadcast(P)),
                    (w_uq[:, 0, :], d_w_uq[l, 0:P].rearrange("r h e -> r (h e)")),
                    (w_uq[0:Q_LORA - P, 1, :], d_w_uq[l, P:Q_LORA].rearrange("r h e -> r (h e)")),
                    (w_ukv, d_w_ukv[l].rearrange("r h e -> r (h e)")),
                ]
                for g in range(A_GROUPS):
                    half = 64 * (g % 2)
                    side.append((bias_s[half:half + 64, g // 2, :], a_b_s[l, g].partition_broadcast(64)))
                for dst, src in side:
                    sp.dma_start(dst, src).then_inc(side_landed, 16)
                for c in range(C_D, C_FEAT):
                    k0 = 2 * (c - C_D)
                    load(l, c, w_in_v[l, :, k0:k0 + 2, COL_D:COL_D + D_IN])
                for c in range(C_FEAT, C_GATE):
                    col = COL_C + 256 * (c - C_FEAT) if c < C_GATE - 1 else 0
                    load(l, c, w_in_v[l, :, :, col:col + 256])
                sp.wait_ge(xn_ready, nth(l, 4, 1))
                sp.dma_start(gain_pre, g_pre_mlp[l].partition_broadcast(P)).then_inc(gain_pre_landed, 16)
                sp.dma_start(gain_post, g_post_mix[l].partition_broadcast(P)).then_inc(gain_post_landed, 16)
                for c in range(C_GATE, C_BRANCH):
                    col = COL_GATE + 256 * (c - C_GATE)
                    load(l, c, w_in_v[l, :, :, col:col + 256])
                for c in range(C_BRANCH, C_OUT):
                    load(l, c, w_br_v[l, c - C_BRANCH])
                for c in range(C_OUT, C_MLP):
                    load(l, c, w_out_v[l, c - C_OUT])
                load(l, C_MLP, mlp_in_v[l, 0])
                load(l, C_MLP + 1, mlp_in_v[l, 1])
                load(l, C_MLP + 2, mlp_out_v[l, 0])
                with sp.Fori(0, PAIRS) as i:
                    for b in range(2):
                        c = C_MLP + 3 + 2 * b
                        load(l, c, mlp_in_loop[l, i, b], i)
                        load(l, c + 1, mlp_out_loop[l, i, b], i)
                load(l, CHUNKS - 1, mlp_out_v[l, STEPS - 1])
                sp.wait_ge(y_scaled, nth(l, 4, 1))
                sp.dma_start(gain_post, g_post_mlp[l].partition_broadcast(P)).then_inc(gain_post_landed, 16)
            for t in range(T):
                sp.wait_ge(x_updated, 4 + nth(L - 1, 4, 2 + t))
                sp.dma_start(out_v[t], x[:, t, :]).then_inc(stored, 16)
            sp.wait_ge(stored, 16 * T)

        @block.scalar
        def _(act):
            def split(l, c, i=0):
                act.wait_ge(raw_landed[c % RAW], 16 * (l * (CHUNKS // RAW) + i * (4 // RAW) + c // RAW + 1))
                act.wait_ge(chunk_used, nth(l, CHUNKS, c + 4 * i))
                n = size_of(c)
                nc.scalar.copy(w_hi[:, c % RING, 0:n], raw[:, c % RAW, 0:n]).then_inc(hi_ready, 1)

            def x_squares(l, k, t):
                act.wait_ge(x_updated, 4 + l * 4 + 2 * k + t - 1)
                nc.scalar.activation(xn[:, t, :], x[:, t, :], ACT.Square, scale=float(D) ** -0.5,
                                     accum_out=ss[:, t:t + 1]).then_inc(ss_ready, 1)

            def xT_evacuate(l, k, t):
                for b in range(2):
                    n = 4 * k + 2 * t + b
                    act.wait_ge(xT_psum, nth(l, 8, n))
                    nc.scalar.copy(xT_hi[:, 4 * b:4 * b + 4, t * P:(t + 1) * P],
                                   psum[:, 4 + 2 * t + b, :].rearrange("p (k n) -> p k n", k=4)
                                   ).then_inc(xT_hi_ready, 1)

            def y_squares(l, t):
                nc.scalar.activation(xn[:, t, :], psum[:, 2 * t:2 * t + 2, :].rearrange("p b n -> p (b n)"),
                                     ACT.Square, scale=float(D) ** -0.5,
                                     accum_out=ss[:, t + 2:t + 3]).then_inc(ss_ready, 1)

            def gate_tanh(l, g):
                act.wait_ge(chunk_used, used(l, C_GATE + g))
                nc.scalar.activation(gate_v[:, g // 4, g % 4, :], psum[:, 6 + g % 2, :], ACT.Tanh,
                                     scale=0.5).then_inc(gate_ready, 1)

            def head_exp(l, h):
                for t in range(T):
                    act.wait_ge(scores_masked, nth(l, 16, 2 * h + t))
                    part = probs[:, h % 2, 0:P] if t == 0 else probs[:, h % 2, P:3 * P]
                    nc.scalar.activation(part, part, ACT.Exp, bias=neg_max[:, h % 2, t:t + 1], scale=-1.0,
                                         accum_out=row_sum[:, h // 4, t, h % 4:h % 4 + 1]).then_inc(probs_ready, 1)

            def head_copy(l, h):
                act.wait_ge(probsT_psum, nth(l, 8, h))
                nc.scalar.copy(probsT[:, h % 2, :], psum[:, 2, 0:3 * P]).then_inc(probsT_copied, 1)

            def branch_hi(l, i, src):
                nc.scalar.copy(brT_hi[:, FT * i:FT * i + FT, :].rearrange("p f n -> p (f n)"), src
                               ).then_inc(brT_hi_ready, 1)

            def side_step(l, s):
                if s == 4:
                    act.wait_ge(vec_psum, nth(l, 1, 0))
                    nc.scalar.copy(vec_cols, psum[:, 6, 0:9]).then_inc(vec_copied, 1)
                    act.wait_ge(wsT_psum, nth(l, 1, 0))
                    nc.scalar.copy(w_sT.rearrange("p g t -> p (g t)"), psum[:, 7, :]).then_inc(wsT_copied, 1)
                    act.wait_ge(proj_copied, nth(l, 4, 3))
                    nc.scalar.activation(av_tmp, proj[:, :, 0:MIX], ACT.Square).then_inc(av_squared, 1)
                if s == 5:
                    act.wait_ge(av_inner, nth(l, 1, 0))
                    nc.scalar.activation(av_tmp, av_tmp, ACT.Tanh, scale=GELU_SCALE).then_inc(av_tanh, 1)
                if s == 6:
                    for n, dst in enumerate((qTB, kTB)):
                        act.wait_ge(qkTB_psum, nth(l, 2, n))
                        nc.scalar.copy(dst.rearrange("p f n -> p (f n)"), psum[:, 6 + n, :]).then_inc(qkTB_copied, 1)
                if s == 8:
                    act.wait_ge(chunk_used, used(l, C_FEAT - 1))
                    for t in range(T):
                        nc.scalar.copy(d_in[:, t, :], psum[:, 4 + t, 0:D_IN]).then_inc(d_in_copied, 1)
                    act.wait_ge(d_in_copied, nth(l, 2, 1))
                    for t in range(T):
                        for n, (a, b) in enumerate(((0, Q_LORA), (Q_LORA, Q_LORA + KV_LORA))):
                            nc.scalar.activation(psum[:, 4 + t, a:b], psum[:, 4 + t, a:b], ACT.Square,
                                                 scale=float(b - a) ** -0.5, accum_out=ssD[:, n, t:t + 1]).then_inc(ssD_ready, 1)
                if s == 10:
                    act.wait_ge(d_latentT_psum, nth(l, 1, 0))
                    act.wait_ge(vec_copied, nth(l, 1, 0))
                    nc.scalar.activation(cqT[:, 0, :], psum[:, 4, 0:S], ACT.Copy, scale=vec_cols[:, 6:7])
                    nc.scalar.activation(ckvT, psum[:, 4, S:2 * S], ACT.Copy, scale=vec_cols[:, 8:9])
                    nc.scalar.activation(cqT[0:Q_LORA - P, 1, :], psum[0:Q_LORA - P, 5, 0:S], ACT.Copy,
                                         scale=vec_cols[0:Q_LORA - P, 7:8]).then_inc(d_latentT_copied, 1)
                if s == 11:
                    for t in range(T):
                        act.wait_ge(qD_psum, nth(l, 2, t))
                        nc.scalar.copy(qD[:, t].rearrange("p h e -> p (h e)"), psum[:, 4 + t, 0:HEADS * QK])
                    for t in range(T):
                        act.wait_ge(kvD_psum, nth(l, 2, t))
                        kv = psum[:, 6 + t, :].rearrange("p (h e) -> p h e", h=HEADS)
                        nc.scalar.copy(kD[:, t, :, 0:D_NOPE], kv[:, :, 0:D_NOPE])
                        last = nc.scalar.copy(vD[:, t, :].rearrange("p (h e) -> p h e", h=HEADS),
                                              kv[:, :, D_NOPE:D_NOPE + D_V])
                    last.then_inc(qkvD_copied, 1)
                if s == 12:
                    act.wait_ge(chunk_used, used(l, C_GATE - 1))
                    nc.scalar.activation(u_tmp, psum[:, 3, :], ACT.Square).then_inc(u_squared, 1)
                if s == 13:
                    act.wait_ge(u_inner, nth(l, 1, 0))
                    nc.scalar.activation(u_tmp, u_tmp, ACT.Tanh, scale=GELU_SCALE).then_inc(u_tanh, 1)
                if s in (13, 14):
                    for n in range(2):
                        j = 2 * (s - 13) + n
                        act.wait_ge(qkTD_psum, nth(l, 4, j))
                        dst = (qTD, kTD)[j // 2][0:QK, 2 * (j % 2):2 * (j % 2) + 2, :]
                        nc.scalar.copy(dst, psum[0:QK, 4 + n, :].rearrange("p (h n) -> p h n", h=2)
                                       ).then_inc(qkTD_copied, 1)
                if s == 14:
                    act.wait_ge(c_out_ready, nth(l, 1, 0))
                    branch_hi(l, 2, conv.rearrange("p f n -> p (f n)"))
                if 15 <= s < 23:
                    head_copy(l, s - 15)
                if 14 <= s < 22:
                    head_exp(l, s - 14)
                if s == 16:
                    act.wait_ge(a_out_ready, nth(l, 1, 0))
                    branch_hi(l, 0, a_out)
                if s in (20, 24):
                    n = (s - 20) // 4
                    act.wait_ge(attnT_psum, nth(l, 2, n))
                    branch_hi(l, (1, 3)[n], psum[:, 4, :])
                if C_GATE < s <= C_BRANCH:
                    gate_tanh(l, s - C_GATE - 1)

            with act.Fori(0, L) as l:
                for t in range(T):
                    x_squares(l, 0, t)
                split(l, 0)
                xT_evacuate(l, 0, 0)
                split(l, 1)
                split(l, 2)
                xT_evacuate(l, 0, 1)
                split(l, 3)
                for t in range(T):
                    for g in range(2):
                        if t == 0:
                            act.wait_ge(proj0_psum, nth(l, 2, g))
                        else:
                            act.wait_ge(chunk_used, used(l, 2 * g + 1))
                        nc.scalar.copy(proj[:, t, 512 * g:512 * g + 512], psum[:, 2 * t + g, :]
                                       ).then_inc(proj_copied, 1)
                        if t == 1:
                            split(l, 4 + 2 * g)
                            if g == 0:
                                split(l, 5)
                for s in range(4, C_OUT):
                    side_step(l, s)
                    split(l, s + 3)
                for u in range(4):
                    act.wait_ge(unit_added, nth(l, 12, 8 + u))
                    nc.scalar.activation(xT_hi[:, 2 * u:2 * u + 2, :].rearrange("p k n -> p (k n)"),
                                         merged[:, u, :], ACT.Copy, scale=0.5).then_inc(mergedT_hi_ready, 1)
                split(l, C_OUT + 3)
                act.wait_ge(y0_psum, nth(l, 2, 0))
                y_squares(l, 0)
                x_squares(l, 1, 0)
                split(l, C_MLP)
                act.wait_ge(chunk_used, used(l, C_MLP - 1))
                y_squares(l, 1)
                split(l, C_MLP + 1)
                xT_evacuate(l, 1, 0)
                x_squares(l, 1, 1)
                split(l, C_MLP + 2)
                xT_evacuate(l, 1, 1)

                def hidden_hi(k, c, i=0):
                    act.wait_ge(chunk_used, used(l, c + 4 * i))
                    nc.scalar.activation(hidden_relu[:, k % 2, :], psum[:, 4 + k % 2, :], ACT.Relu
                                         ).then_inc(relu_ready, 1)
                    act.wait_ge(relu_ready, nth(l, STEPS, k + 2 * i))
                    nc.scalar.activation(brT_hi[:, 2 * (k % 2):2 * (k % 2) + 2, :].rearrange("p f n -> p (f n)"),
                                         hidden_relu[:, k % 2, :], ACT.Square).then_inc(hidden_hi_ready, 1)

                split(l, C_MLP + 3)
                hidden_hi(0, C_MLP)
                with act.Fori(0, PAIRS) as i:
                    for b in range(2):
                        m = C_MLP + 1 + 2 * b
                        split(l, m + 3, i)
                        hidden_hi(1 + b, m, i)
                        split(l, m + 4, i)
                hidden_hi(STEPS - 1, CHUNKS - 3)
                act.wait_ge(y0_psum, nth(l, 2, 1))
                y_squares(l, 0)
                act.wait_ge(chunk_used, used(l, CHUNKS - 1))
                y_squares(l, 1)

        @block.vector
        def _(dve):
            v = nc.vector

            def split(l, c, i=0):
                dve.wait_ge(hi_ready, nth(l, CHUNKS, c + 4 * i))
                n = size_of(c)
                v.tensor_tensor(w_lo[:, c % RING, 0:n], raw[:, c % RAW, 0:n],
                                w_hi[:, c % RING, 0:n].bitcast(F32), ALU.subtract).then_inc(lo_ready, 1)

            def normalise(l, k, t):
                if k == 0 or t == 0:
                    dve.wait_ge(gain_pre_landed, 16 * nth(l, 2, k))
                dve.wait_ge(rstd_ready, nth(l, 8, (0, 1, 3, 5)[2 * k + t]))
                v.scalar_tensor_tensor(xn[:, t, :], x[:, t, :], rstd[:, t:t + 1], gain_pre,
                                       ALU.mult, ALU.mult).then_inc(xn_ready, 1)

            def xT_evacuate(l, k, t):
                for b in range(2):
                    n = 4 * k + 2 * t + b
                    dve.wait_ge(xT_hi_ready, nth(l, 8, n))
                    cut = slice(t * P, (t + 1) * P)
                    v.tensor_tensor(xT_lo[:, 4 * b:4 * b + 4, cut],
                                    psum[:, 4 + 2 * t + b, :].rearrange("p (k n) -> p k n", k=4),
                                    xT_hi[:, 4 * b:4 * b + 4, cut].bitcast(F32), ALU.subtract
                                    ).then_inc(xT_lo_ready, 1)

            def residual(l, k, t):
                if t == 0:
                    dve.wait_ge(gain_post_landed, 16 * nth(l, 2, k))
                dve.wait_ge(rstd_ready, nth(l, 8, (2, 4, 6, 7)[2 * k + t]))
                v.scalar_tensor_tensor(xn[:, t, :], psum[:, 2 * t:2 * t + 2, :].rearrange("p b n -> p (b n)"),
                                       rstd[:, t + 2:t + 3], gain_post, ALU.mult, ALU.mult).then_inc(y_scaled, 1)
                dve.wait_ge(y_scaled, nth(l, 4, 2 * k + t))
                v.tensor_tensor(x[:, t, :], x[:, t, :], xn[:, t, :], ALU.add).then_inc(x_updated, 1)

            def rope(l, x1, x2, cos, sin, shape, products, n, per_layer):
                size = 1
                for d in shape[1:]:
                    size *= d
                names = "abcd"[:len(shape) - 1]
                sizes = {names[i]: shape[i + 1] for i in range(len(names) - 1)}
                tmp = [rope_tmp[:, i, 0:size].rearrange(f"p ({' '.join(names)}) -> p {' '.join(names)}", **sizes)
                       for i in range(4)]
                v.tensor_tensor(tmp[0], x1, cos, ALU.mult)
                v.tensor_tensor(tmp[1], x2, sin, ALU.mult)
                v.tensor_tensor(tmp[2], x2, cos, ALU.mult)
                v.tensor_tensor(tmp[3], x1, sin, ALU.mult).then_inc(products, 1)
                dve.wait_ge(products, nth(l, per_layer, n))
                return tmp

            def table(offset, half, shape):
                t = tables[:, :, offset:offset + half]
                return t.unsqueeze(2).broadcast_to(shape) if len(shape) == 4 else t

            def head_mask(l, h):
                scale = -(float(HD) ** -0.5 if h < 4 else float(QK) ** -0.5)
                dve.wait_ge(scores_psum, nth(l, 8, h))
                bank = psum[:, h % 2, :]
                apart(dve)
                v.tensor_tensor_reduce(probs[:, h % 2, 0:P], bank[:, 0:P], causal[:, P:2 * P], scale, 3.0e38,
                                       ALU.add, ALU.min, neg_max[:, h % 2, 0:1]).then_inc(scores_masked, 1)
                v.tensor_tensor_reduce(probs[:, h % 2, P:3 * P], bank[:, P:3 * P], causal, scale, 3.0e38,
                                       ALU.add, ALU.min, neg_max[:, h % 2, 1:2]).then_inc(scores_masked, 1)

            def branch_lo(l, i, order, src):
                dve.wait_ge(brT_hi_ready, nth(l, 4, order))
                flat = "p f n -> p (f n)"
                v.tensor_tensor(brT_lo[:, FT * i:FT * i + FT, :].rearrange(flat), src,
                                brT_hi[:, FT * i:FT * i + FT, :].rearrange(flat).bitcast(F32), ALU.subtract
                                ).then_inc(brT_lo_ready, 1)

            def side_step(l, s):
                if s == 4:
                    dve.wait_ge(proj_copied, nth(l, 4, 3))
                    qk = proj[:, :, MIX:3 * MIX].rearrange("p t (h e) -> p t h e", e=HD)
                    h = B_ROT // 2
                    shape = [P, T, 2 * HEADS, h]
                    x1, x2 = qk[:, :, :, 0:h], qk[:, :, :, h:2 * h]
                    tmp = rope(l, x1, x2, table(0, h, shape), table(h, h, shape), shape,
                               ropeB_products, 0, 1)
                    v.tensor_tensor(x1, tmp[0], tmp[1], ALU.subtract)
                    v.tensor_tensor(x2, tmp[2], tmp[3], ALU.add).then_inc(ropeB_ready, 1)
                if s == 5:
                    dve.wait_ge(av_squared, nth(l, 1, 0))
                    v.tensor_scalar(av2, av_tmp, GELU_CUBE, 1.0, ALU.mult, ALU.add).then_inc(av_poly, 1)
                    dve.wait_ge(av_poly, nth(l, 1, 0))
                    v.tensor_tensor(av_tmp, av2, proj[:, :, 0:MIX], ALU.mult).then_inc(av_inner, 1)
                if s == 6:
                    dve.wait_ge(av_tanh, nth(l, 1, 0))
                    v.scalar_tensor_tensor(av2, av_tmp, 1.0, proj[:, :, 0:MIX], ALU.add, ALU.mult
                                           ).then_inc(av_gelu, 1)
                    dve.wait_ge(av_gelu, nth(l, 1, 0))
                    for t in range(T):
                        v.bn_stats(ln_stats[:, t, :], av2[:, t, :]).then_inc(ln_stats_ready, 1)
                    dve.wait_ge(ln_stats_ready, nth(l, 2, 1))
                    apart(dve)
                    for t in range(T):
                        v.bn_aggr(ln_mv[:, t, :], ln_stats[:, t, :]).then_inc(ln_mv_ready, 1)
                if s == 7:
                    dve.wait_ge(ln_rstd_ready, nth(l, 1, 0))
                    for t in range(T):
                        v.tensor_scalar(av2[:, t, :], av2[:, t, :], ln_mv[:, t, 0:1], ln_rstd[:, t:t + 1],
                                        ALU.subtract, ALU.mult).then_inc(ln_centred, 1)
                    dve.wait_ge(ln_centred, nth(l, 2, 1))
                    dve.wait_ge(side_landed, 16 * nth(l, 14, 13))
                    wide = [P, T, MIX]
                    v.tensor_tensor(av2, av2, ln_g.unsqueeze(1).broadcast_to(wide), ALU.mult).then_inc(ln_scaled, 1)
                    dve.wait_ge(ln_scaled, nth(l, 1, 0))
                    v.tensor_tensor(av2, av2, ln_b.unsqueeze(1).broadcast_to(wide), ALU.add).then_inc(ln_ready, 1)
                if s == 11:
                    dve.wait_ge(chunk_used, used(l, C_FEAT + 2))
                    banks = [psum[:, b, :].rearrange("p (f n) -> p f n", f=FT) for b in range(3)]
                    v.memset(z[:, :, 0:2], 0.0)
                    v.tensor_copy(conv, banks[1]).then_inc(z_ready, 1)
                    dve.wait_ge(z_ready, nth(l, 2, 0))
                    v.tensor_tensor(z[:, :, 2:S + 2], conv, banks[2], ALU.mult).then_inc(z_ready, 1)
                    dve.wait_ge(z_ready, nth(l, 2, 1))
                    dve.wait_ge(vec_copied, nth(l, 1, 0))
                    for f in range(FT):
                        last = v.tensor_scalar(conv[:, f, :], z[:, f, 2:S + 2], vec_cols[:, 4 + f:5 + f], None,
                                               ALU.mult)
                    last.then_inc(conv_tap, 1)
                    for k in (1, 0):
                        dve.wait_ge(conv_tap, nth(l, 3, 1 - k))
                        for f in range(FT):
                            last = v.scalar_tensor_tensor(conv[:, f, :], z[:, f, k:S + k],
                                                          vec_cols[:, 2 * k + f:2 * k + f + 1], conv[:, f, :],
                                                          ALU.mult, ALU.add)
                        last.then_inc(conv_tap, 1)
                    dve.wait_ge(conv_tap, nth(l, 3, 2))
                    v.tensor_tensor(conv, conv, banks[0], ALU.mult).then_inc(c_out_ready, 1)
                if s == 12:
                    dve.wait_ge(qkvD_copied, nth(l, 1, 0))
                    h, o = D_ROPE // 2, B_ROT
                    shape = [P, T, HEADS, h]
                    x1, x2 = qD[:, :, :, D_NOPE:D_NOPE + h], qD[:, :, :, D_NOPE + h:QK]
                    tmp = rope(l, x1, x2, table(o, h, shape), table(o + h, h, shape), shape,
                               ropeD_products, 0, 2)
                    v.tensor_tensor(x1, tmp[0], tmp[1], ALU.subtract)
                    v.tensor_tensor(x2, tmp[2], tmp[3], ALU.add).then_inc(ropeD_ready, 1)
                    dve.wait_ge(ropeD_ready, nth(l, 2, 0))
                    kr = d_in[:, :, Q_LORA + KV_LORA:D_IN]
                    tmp = rope(l, kr[:, :, 0:h], kr[:, :, h:D_ROPE], table(o, h, [P, T, h]),
                               table(o + h, h, [P, T, h]), [P, T, h], ropeD_products, 1, 2)
                    tmp = [a.unsqueeze(2).broadcast_to(shape) for a in tmp]
                    v.tensor_tensor(kD[:, :, :, D_NOPE:D_NOPE + h], tmp[0], tmp[1], ALU.subtract)
                    v.tensor_tensor(kD[:, :, :, D_NOPE + h:QK], tmp[2], tmp[3], ALU.add).then_inc(ropeD_ready, 1)
                    dve.wait_ge(u_squared, nth(l, 1, 0))
                    v.tensor_scalar(u2, u_tmp, GELU_CUBE, 1.0, ALU.mult, ALU.add).then_inc(u_poly, 1)
                    dve.wait_ge(u_poly, nth(l, 1, 0))
                    v.tensor_tensor(u_tmp, u2, psum[:, 3, :], ALU.mult).then_inc(u_inner, 1)
                if s == 13:
                    dve.wait_ge(u_tanh, nth(l, 1, 0))
                    v.scalar_tensor_tensor(u2, u_tmp, 1.0, psum[:, 3, :], ALU.add, ALU.mult).then_inc(u_gelu, 1)
                if s == 14:
                    branch_lo(l, 2, ORDER_C, conv.rearrange("p f n -> p (f n)"))
                if 14 <= s < 22:
                    head_mask(l, s - 14)
                if s == 15:
                    dve.wait_ge(sv_psum, nth(l, 1, 0))
                    dve.wait_ge(u_gelu, nth(l, 1, 0))
                    four = [P, FT, T, P]
                    sv = psum[:, 4, :].rearrange("p (f t n) -> p f t n", f=FT, t=T)
                    v.tensor_tensor(a_out.rearrange("p (f t n) -> p f t n", f=FT, t=T), sv,
                                    bias_s.unsqueeze(2).broadcast_to(four), ALU.add).then_inc(sv_biased, 1)
                    dve.wait_ge(sv_biased, nth(l, 1, 0))
                    v.scalar_tensor_tensor(a_out, u2, 0.5, a_out, ALU.mult, ALU.mult).then_inc(a_out_ready, 1)
                if s == 16:
                    branch_lo(l, 0, ORDER_A, a_out)
                if s in (19, 23):
                    n = (s - 19) // 4
                    dve.wait_ge(probs_ready, nth(l, 16, 8 * n + 7))
                    v.reciprocal(inv_sum[:, n], row_sum[:, n]).then_inc(inv_sum_ready, 1)
                    dve.wait_ge(inv_sum_ready, nth(l, 2, n))
                    dve.wait_ge(attn_psum, nth(l, 8, 4 * n + 3))
                    four = [P, T, HEADS, HD]
                    bank = psum[:, (3, 5)[n], :].rearrange("p (t h e) -> p t h e", t=T, h=HEADS)
                    v.tensor_tensor(o_sb.rearrange("p t (h e) -> p t h e", h=HEADS), bank,
                                    inv_sum[:, n].unsqueeze(3).broadcast_to(four), ALU.mult
                                    ).then_inc(attn_ready, 1)
                if s in (20, 24):
                    n = (s - 20) // 4
                    branch_lo(l, (1, 3)[n], (ORDER_B, ORDER_D)[n], psum[:, 4, :])
                if C_BRANCH < s <= C_OUT:
                    gate_units(l, s - C_BRANCH - 1)

            def gate_units(l, i):
                for u in range(4):
                    if u < 3:
                        dve.wait_ge(unit_psum, nth(l, 12, 3 * i + u))
                    else:
                        dve.wait_ge(chunk_used, used(l, C_BRANCH + i))
                    if i == 0:
                        dve.wait_ge(gate_ready, nth(l, 16, 15))
                    if i >= 2:
                        dve.wait_ge(unit_added, nth(l, 12, 4 * (i - 2) + u))
                    dst = merged[:, u, :] if i == 0 else gated[:, u, :]
                    v.scalar_tensor_tensor(dst, gate_v[:, i, u, :], 1.0, psum[:, 4 + u, :], ALU.add, ALU.mult
                                           ).then_inc(unit_gated, 1)

            v.memset(start_mark[:, 0:1], 0.0).then_inc(lo_ready, RING)
            v.memset(start_mark[:, 1:2], 0.0).then_inc(chunk_used, RING)
            dve.wait_ge(x_landed, 16 * T)
            v.memset(start_mark[:, 2:3], 0.0).then_inc(x_updated, 4)
            with dve.Fori(0, L) as l:
                normalise(l, 0, 0)
                normalise(l, 0, 1)
                split(l, 0)
                xT_evacuate(l, 0, 0)
                split(l, 1)
                split(l, 2)
                xT_evacuate(l, 0, 1)
                for c in range(3, 7):
                    split(l, c)
                dve.wait_ge(tables_landed, 16)
                for s in range(4, C_OUT):
                    side_step(l, s)
                    if s == 8:
                        split(l, s + 3)
                        dve.wait_ge(rstdD_ready, nth(l, 1, 0))
                        for t in range(T):
                            for n, (a, b) in enumerate(((0, Q_LORA), (Q_LORA, Q_LORA + KV_LORA))):
                                last = v.tensor_scalar(d_in[:, t, a:b], d_in[:, t, a:b], rstdD[:, n, t:t + 1], None,
                                                       ALU.mult)
                        last.then_inc(d_normed, 1)
                    else:
                        split(l, s + 3)
                side_step(l, C_OUT)
                for u in range(4):
                    dve.wait_ge(mergedT_hi_ready, nth(l, 4, u))
                    flat = "p k n -> p (k n)"
                    v.scalar_tensor_tensor(xT_lo[:, 2 * u:2 * u + 2, :].rearrange(flat), merged[:, u, :], 0.5,
                                           xT_hi[:, 2 * u:2 * u + 2, :].rearrange(flat).bitcast(F32),
                                           ALU.mult, ALU.subtract).then_inc(mergedT_lo_ready, 1)
                split(l, C_OUT + 3)
                residual(l, 0, 0)
                split(l, C_MLP)
                normalise(l, 1, 0)
                residual(l, 0, 1)
                xT_evacuate(l, 1, 0)
                normalise(l, 1, 1)
                split(l, C_MLP + 1)
                split(l, C_MLP + 2)
                xT_evacuate(l, 1, 1)

                def hidden(k, i=0):
                    if k >= 1:
                        dve.wait_ge(hidden_lo_ready, nth(l, STEPS, k - 1 + 2 * i))
                    dve.wait_ge(relu_ready, nth(l, STEPS, k + 2 * i))
                    v.tensor_tensor(hidden_sq, hidden_relu[:, k % 2, :], hidden_relu[:, k % 2, :], ALU.mult
                                    ).then_inc(hidden_squared, 1)
                    dve.wait_ge(hidden_squared, nth(l, STEPS, k + 2 * i))
                    dve.wait_ge(hidden_hi_ready, nth(l, STEPS, k + 2 * i))
                    flat = "p f n -> p (f n)"
                    half = slice(2 * (k % 2), 2 * (k % 2) + 2)
                    v.tensor_tensor(brT_lo[:, half, :].rearrange(flat), hidden_sq,
                                    brT_hi[:, half, :].rearrange(flat).bitcast(F32), ALU.subtract
                                    ).then_inc(hidden_lo_ready, 1)

                split(l, C_MLP + 3)
                hidden(0)
                with dve.Fori(0, PAIRS) as i:
                    for b in range(2):
                        m = C_MLP + 1 + 2 * b
                        split(l, m + 3, i)
                        hidden(1 + b, i)
                        split(l, m + 4, i)
                hidden(STEPS - 1)
                residual(l, 1, 0)
                residual(l, 1, 1)

        @block.gpsimd
        def _(pool):
            g = nc.gpsimd
            sp_tables = rope_tables.rearrange("(t p) n -> p t n", p=P)
            pool.dma_start(tables, sp_tables).then_inc(tables_landed, 16)
            g.memset(ident, 0.0).then_inc(consts_ready, 1)
            g.memset(causal, 0.0).then_inc(consts_ready, 1)
            g.memset(minus_half, -0.5).then_inc(consts_ready, 1)
            g.memset(vec_rows, 0.0).then_inc(consts_ready, 1)
            g.memset(norm_eps, NORM_EPS).then_inc(consts_ready, 1)
            g.memset(ln_eps, 4 * LN_EPS).then_inc(consts_ready, 1)
            pool.wait_ge(consts_ready, 6)
            g.affine_select(out=ident, in_=ident, compare_op=ALU.not_equal, fill=1.0, base=0,
                            pattern=[[-1, P]], channel_multiplier=1).then_inc(consts_ready, 1)
            g.affine_select(out=causal[:, P:2 * P], in_=causal[:, P:2 * P], compare_op=ALU.is_ge, fill=MASKED,
                            base=0, pattern=[[-1, P]], channel_multiplier=1).then_inc(consts_ready, 1)

            def inverse_rms(l, n, col):
                pool.wait_ge(ss_ready, nth(l, 8, n))
                g.tensor_tensor(ms[:, col:col + 1], ss[:, col:col + 1], norm_eps[:, 0:1], ALU.add
                                ).then_inc(ms_ready, 1)
                pool.wait_ge(ms_ready, nth(l, 8, n))
                g.tensor_tensor(rstd[:, col:col + 1], ms[:, col:col + 1], minus_half[:, 0:1], ALU.pow
                                ).then_inc(rstd_ready, 1)

            with pool.Fori(0, L) as l:
                for t in range(T):
                    inverse_rms(l, t, t)
                pool.wait_ge(side_landed, 16 * nth(l, 14, 13))
                apart(pool)
                g.affine_select(out=w_s, in_=w_s, compare_op=ALU.is_ge, fill=0.0, base=0,
                                pattern=[[0, A_GROUPS], [-1, P]], channel_multiplier=1).then_inc(ws_masked, 1)
                pool.wait_ge(ln_mv_ready, nth(l, 2, 1))
                g.tensor_tensor(ln_ms, ln_mv[:, :, 1], ln_eps, ALU.add).then_inc(ln_ms_ready, 1)
                pool.wait_ge(ln_ms_ready, nth(l, 1, 0))
                g.tensor_tensor(ln_rstd, ln_ms, minus_half[:, 0:T], ALU.pow).then_inc(ln_rstd_ready, 1)
                pool.wait_ge(ssD_ready, nth(l, 4, 3))
                g.tensor_tensor(msD.rearrange("p n t -> p (n t)"), ssD.rearrange("p n t -> p (n t)"), norm_eps,
                                ALU.add).then_inc(msD_ready, 1)
                pool.wait_ge(msD_ready, nth(l, 1, 0))
                g.tensor_tensor(rstdD.rearrange("p n t -> p (n t)"), msD.rearrange("p n t -> p (n t)"),
                                minus_half, ALU.pow).then_inc(rstdD_ready, 1)
                for i in range(1, NB):
                    for u in range(4):
                        pool.wait_ge(unit_gated, nth(l, 16, 4 * i + u))
                        if i > 1:
                            pool.wait_ge(unit_added, nth(l, 12, 4 * (i - 2) + u))
                        g.tensor_tensor(merged[:, u, :], merged[:, u, :], gated[:, u, :], ALU.add
                                        ).then_inc(unit_added, 1)
                for n, col in enumerate((2, 0, 3, 1, 2, 3)):
                    inverse_rms(l, 2 + n, col)

        @block.tensor
        def _(pe):
            def product(dst, lhs, rhs, first, last):
                (l_hi, l_lo), (r_hi, r_lo) = lhs, rhs
                nc.tensor.matmul(dst, l_hi, r_hi, start=first, stop=False)
                nc.tensor.matmul(dst, l_hi, r_lo, start=False, stop=False)
                return nc.tensor.matmul(dst, l_lo, r_hi, start=False, stop=last)

            def wait_chunk(l, c, i=0):
                pe.wait_ge(lo_ready, split_done(l, c + 4 * i))

            def transpose_x(l, k, t):
                pe.wait_ge(xn_ready, nth(l, 4, 2 * k + t))
                for b in range(2):
                    for j in range(4):
                        kt = 4 * b + j
                        last = nc.tensor.transpose(psum[:, 4 + 2 * t + b, j * P:(j + 1) * P],
                                                   xn[:, t, kt * P:(kt + 1) * P], ident)
                    last.then_inc(xT_psum, 1)

            def xT(kt, cut=slice(0, S)):
                return xT_hi[:, kt, cut], xT_lo[:, kt, cut]

            def tokens(t):
                return slice(t * P, (t + 1) * P)

            def feature_major(l, c, bank):
                hi, lo = both(c)
                for f in range(2):
                    cut = slice(f * P, (f + 1) * P)
                    for kt in range(KT):
                        last = product(psum[:, bank, f * S:(f + 1) * S], (hi[:, kt, cut], lo[:, kt, cut]), xT(kt),
                                       kt == 0, kt == KT - 1)
                return last

            def head_scores(l, h):
                n = h % 4
                if h < 4:
                    part = slice(64 * (n % 2), 64 * (n % 2) + 64)
                    q, k = qTB[part, n // 2, :], kTB[part, n // 2, :]
                else:
                    q, k = qTD[0:QK, n, :], kTD[0:QK, n, :]
                if h == 0:
                    pe.wait_ge(qkTB_copied, nth(l, 2, 1))
                    pe.wait_ge(c_out_ready, nth(l, 1, 0))
                if h == 4:
                    pe.wait_ge(qkTD_copied, nth(l, 4, 3))
                if h >= 2:
                    pe.wait_ge(scores_masked, nth(l, 16, 2 * (h - 2) + 1))
                nc.tensor.matmul(psum[:, h % 2, 0:P], q[:, 0:P], k[:, 0:P], start=True, stop=True)
                nc.tensor.matmul(psum[:, h % 2, P:3 * P], q[:, P:S], k, start=True, stop=True
                                 ).then_inc(scores_psum, 1)

            def head_transpose(l, h):
                pe.wait_ge(probs_ready, nth(l, 16, 2 * h + 1))
                if h >= 1:
                    pe.wait_ge(probsT_copied, nth(l, 8, h - 1))
                for b in range(3):
                    last = nc.tensor.transpose(psum[:, 2, b * P:(b + 1) * P], probs[:, h % 2, b * P:(b + 1) * P],
                                               ident)
                last.then_inc(probsT_psum, 1)

            def head_values(l, h):
                pe.wait_ge(probsT_copied, nth(l, 8, h))
                if h == 0:
                    pe.wait_ge(u_gelu, nth(l, 1, 0))
                if h == 4:
                    pe.wait_ge(qkTD_copied, nth(l, 4, 3))
                n = h % 4
                v = [proj[:, t, 3 * MIX + HD * n:3 * MIX + HD * n + HD] if h < 4 else
                     vD[:, t, D_V * n:D_V * n + D_V] for t in range(T)]
                bank, pT = psum[:, (3, 5)[h // 4], :], probsT[:, h % 2, :]
                nc.tensor.matmul(bank[:, HD * n:HD * n + HD], pT[:, 0:P], v[0], start=True, stop=True)
                o = MIX + HD * n
                nc.tensor.matmul(bank[:, o:o + HD], pT[:, P:2 * P], v[0], start=True, stop=False)
                nc.tensor.matmul(bank[:, o:o + HD], pT[:, 2 * P:3 * P], v[1], start=False, stop=True
                                 ).then_inc(attn_psum, 1)

            def side_after(l, c):
                if c == 3:
                    pe.wait_ge(side_landed, 16 * nth(l, 14, 13))
                    apart(pe)
                    nc.tensor.transpose(psum[:, 6, 0:9], vec_rows, ident[0:9, 0:9]).then_inc(vec_psum, 1)
                    pe.wait_ge(ws_masked, nth(l, 1, 0))
                    for g in range(A_GROUPS):
                        last = nc.tensor.transpose(psum[:, 7, g * P:(g + 1) * P], w_s[:, g, :], ident)
                    last.then_inc(wsT_psum, 1)
                if c == 5:
                    pe.wait_ge(ropeB_ready, nth(l, 1, 0))
                    pe.wait_ge(wsT_copied, nth(l, 1, 0))
                    for n in range(2):
                        for f in range(FT):
                            for t in range(T):
                                o = MIX * (1 + n) + f * P
                                last = nc.tensor.transpose(psum[:, 6 + n, f * S + t * P:f * S + (t + 1) * P],
                                                           proj[:, t, o:o + P], ident)
                        last.then_inc(qkTB_psum, 1)
                if c == 9:
                    pe.wait_ge(d_normed, nth(l, 1, 0))
                    pe.wait_ge(ssD_ready, nth(l, 4, 3))
                    for t in range(T):
                        nc.tensor.transpose(psum[:, 4, t * P:(t + 1) * P], d_in[:, t, 0:P], ident)
                        nc.tensor.transpose(psum[:, 4, S + t * P:S + (t + 1) * P],
                                            d_in[:, t, Q_LORA:Q_LORA + KV_LORA], ident)
                        last = nc.tensor.transpose(psum[0:Q_LORA - P, 5, t * P:(t + 1) * P],
                                                   d_in[:, t, P:Q_LORA], ident)
                    last.then_inc(d_latentT_psum, 1)
                if c == 10:
                    pe.wait_ge(d_latentT_copied, nth(l, 1, 0))
                    pe.wait_ge(qkTB_copied, nth(l, 2, 1))
                    rest = slice(0, Q_LORA - P)
                    for t in range(T):
                        dst = psum[:, 4 + t, 0:HEADS * QK]
                        nc.tensor.matmul(dst, cqT[:, 0, tokens(t)], w_uq[:, 0, :], start=True, stop=False)
                        nc.tensor.matmul(dst, cqT[rest, 1, tokens(t)], w_uq[rest, 1, :], start=False, stop=True
                                         ).then_inc(qD_psum, 1)
                    for t in range(T):
                        nc.tensor.matmul(psum[:, 6 + t, :], ckvT[:, tokens(t)], w_ukv, start=True, stop=True
                                         ).then_inc(kvD_psum, 1)
                if c in (12, 13):
                    n = c - 12
                    pe.wait_ge(ropeD_ready, nth(l, 2, n))
                    pe.wait_ge(qkvD_copied, nth(l, 1, 0))
                    if n == 1:
                        pe.wait_ge(qkTD_copied, nth(l, 4, 1))
                    src = (qD, kD)[n]
                    for b in range(2):
                        for j in range(2):
                            for t in range(T):
                                last = nc.tensor.transpose(psum[0:QK, 4 + b, j * S + t * P:j * S + (t + 1) * P],
                                                           src[:, t, 2 * b + j, :], ident)
                        last.then_inc(qkTD_psum, 1)
                if c == 14:
                    pe.wait_ge(ln_ready, nth(l, 1, 0))
                    pe.wait_ge(qkTD_copied, nth(l, 4, 3))
                    for g in range(A_GROUPS):
                        part = slice(64 * (g % 2), 64 * (g % 2) + 64)
                        for t in range(T):
                            o = (g // 2) * S + t * P
                            last = nc.tensor.matmul(psum[part, 4, o:o + P], av2[:, t, 64 * g:64 * g + 64],
                                                    w_sT[:, g, :], start=True, stop=True)
                    last.then_inc(sv_psum, 1)
                if 13 <= c < 21:
                    head_scores(l, c - 13)
                if 14 <= c < 22:
                    head_transpose(l, c - 14)
                if 15 <= c < 23:
                    head_values(l, c - 15)
                if c in (19, 23):
                    n = (c - 19) // 4
                    pe.wait_ge(attn_ready, nth(l, 2, n))
                    if n == 0:
                        pe.wait_ge(a_out_ready, nth(l, 1, 0))
                    else:
                        pe.wait_ge(brT_lo_ready, nth(l, 4, ORDER_B))
                    for f in range(FT):
                        for t in range(T):
                            last = nc.tensor.transpose(psum[:, 4, f * S + t * P:f * S + (t + 1) * P],
                                                       o_sb[:, t, f * P:(f + 1) * P], ident)
                    last.then_inc(attnT_psum, 1)

            pe.wait_ge(consts_ready, CONSTS)
            with pe.Fori(0, L) as l:
                for t in range(T):
                    transpose_x(l, 0, t)
                for t in range(T):
                    for c in range(C_D):
                        g, kh = c // 2, c % 2
                        wait_chunk(l, c)
                        if g == 0:
                            pe.wait_ge(xT_lo_ready, nth(l, 8, 2 * t + kh))
                        hi, lo = both(c)
                        for j in range(4):
                            kt = 4 * kh + j
                            last = product(psum[:, 2 * t + g, :], xT(kt, tokens(t)), (hi[:, j, :], lo[:, j, :]),
                                           kt == 0, kt == KT - 1)
                        if t == 1:
                            last.then_inc(chunk_used, 1)
                        elif kh == 1:
                            last.then_inc(proj0_psum, 1)
                side_after(l, 3)
                for c in range(C_D, C_FEAT):
                    wait_chunk(l, c)
                    hi, lo = both(c)
                    for t in range(T):
                        for j in range(2):
                            kt = 2 * (c - C_D) + j
                            last = product(psum[:, 4 + t, 0:D_IN], xT(kt, tokens(t)), (hi[:, j, :], lo[:, j, :]),
                                           kt == 0, kt == KT - 1)
                    last.then_inc(chunk_used, 1)
                    side_after(l, c)
                pe.wait_ge(proj_copied, nth(l, 4, 3))
                for c in range(C_FEAT, C_GATE):
                    wait_chunk(l, c)
                    feature_major(l, c, c - C_FEAT).then_inc(chunk_used, 1)
                    side_after(l, c)
                pe.wait_ge(qkvD_copied, nth(l, 1, 0))
                for c in range(C_GATE, C_BRANCH):
                    n = c - C_GATE
                    wait_chunk(l, c)
                    if n >= 2:
                        pe.wait_ge(gate_ready, nth(l, 16, n - 2))
                    feature_major(l, c, 6 + n % 2).then_inc(chunk_used, 1)
                    side_after(l, c)
                for i in range(NB):
                    c = C_BRANCH + i
                    wait_chunk(l, c)
                    if i == 0:
                        pe.wait_ge(brT_lo_ready, nth(l, 4, ORDER_D))
                        pe.wait_ge(gate_ready, nth(l, 16, 15))
                    hi, lo = both(c)
                    for u in range(4):
                        if i >= 1:
                            pe.wait_ge(unit_gated, nth(l, 16, 4 * (i - 1) + u))
                        for f in range(2):
                            cut = slice((2 * u + f) * P, (2 * u + f + 1) * P)
                            for kt in range(FT):
                                last = product(psum[:, 4 + u, f * S:(f + 1) * S], (hi[:, kt, cut], lo[:, kt, cut]),
                                               (brT_hi[:, FT * i + kt, :], brT_lo[:, FT * i + kt, :]),
                                               kt == 0, kt == FT - 1)
                        last.then_inc(unit_psum if u < 3 else chunk_used, 1)
                for t in range(T):
                    for c in range(C_OUT, C_MLP):
                        wait_chunk(l, c)
                        if t == 0:
                            pe.wait_ge(mergedT_lo_ready, nth(l, 4, c - C_OUT))
                        hi, lo = both(c)
                        for half in range(2):
                            cut = slice(512 * half, 512 * half + 512)
                            for j in range(2):
                                kt = 2 * (c - C_OUT) + j
                                last = product(psum[:, 2 * t + half, :], xT(kt, tokens(t)),
                                               (hi[:, j, cut], lo[:, j, cut]), kt == 0, kt == KT - 1)
                        if t == 1:
                            last.then_inc(chunk_used, 1)
                    if t == 0:
                        last.then_inc(y0_psum, 1)
                for t in range(T):
                    transpose_x(l, 1, t)

                def mlp_in(k, c, i=0):
                    wait_chunk(l, c, i)
                    feature_major(l, c, 4 + k % 2).then_inc(chunk_used, 1)

                def mlp_out(k, c, i=0, first=False, last=False):
                    wait_chunk(l, c, i)
                    pe.wait_ge(hidden_lo_ready, nth(l, STEPS, k + 2 * i))
                    hi, lo = both(c)
                    for t in range(T):
                        for half in range(2):
                            cut = slice(512 * half, 512 * half + 512)
                            for j in range(2):
                                n = 2 * (k % 2) + j
                                mm = product(psum[:, 2 * t + half, :],
                                             (brT_hi[:, n, tokens(t)], brT_lo[:, n, tokens(t)]),
                                             (hi[:, j, cut], lo[:, j, cut]), first and j == 0, last and j == 1)
                        if t == 1:
                            mm.then_inc(chunk_used, 1)
                        elif last:
                            mm.then_inc(y0_psum, 1)

                pe.wait_ge(xT_lo_ready, nth(l, 8, 7))
                mlp_in(0, C_MLP)
                mlp_in(1, C_MLP + 1)
                mlp_out(0, C_MLP + 2, first=True)
                with pe.Fori(0, PAIRS) as i:
                    for b in range(2):
                        pe.wait_ge(relu_ready, nth(l, STEPS, b + 2 * i))
                        mlp_in(2 + b, C_MLP + 3 + 2 * b, i)
                        mlp_out(1 + b, C_MLP + 4 + 2 * b, i)
                mlp_out(STEPS - 1, CHUNKS - 1, last=True)


_INS = ['x', 'g_pre_mix', 'w_in', 'a_ln_g', 'a_ln_b', 'a_w_s', 'a_b_s', 'c_w_conv', 'd_q_norm_g', 'd_w_uq',
        'd_kv_norm_g', 'd_w_ukv', 'w_branch', 'w_out', 'g_post_mix', 'g_pre_mlp', 'w_mlp_in', 'w_mlp_out',
        'g_post_mlp']
ROPE_THETA = 500000.0


def _rope_tables(seq):
    import numpy as np
    parts = []
    for dim in (B_ROT, D_ROPE):
        exponent = np.arange(0, dim, 2, dtype=np.float32) / np.float32(dim)
        inv = np.float32(1.0) / np.power(np.float64(ROPE_THETA), exponent).astype(np.float32)
        angle = np.arange(seq, dtype=np.float32)[:, None] * inv[None, :]
        parts += [np.cos(angle.astype(np.float64)), np.sin(angle.astype(np.float64))]
    return np.concatenate(parts, axis=1).astype(np.float32)


def kernel(**inputs):
    import numpy as _np
    import concourse.bacc as _bacc
    from concourse import mybir as _mybir
    from concourse.bass_utils import run_bass_kernel_spmd as _run

    nc = _bacc.Bacc("TRN2", target_bir_lowering=False, num_devices=1)
    arrays, args = {}, []
    shape = _np.shape(inputs['x'])
    for name, a in [(n, inputs[n]) for n in _INS] + [('rope_tables', _rope_tables(shape[1]))]:
        a = _np.ascontiguousarray(a)
        arrays[f"in_{name}_dram"] = a
        args.append(nc.dram_tensor(f"in_{name}_dram", a.shape, _mybir.dt.from_np(a.dtype), kind="ExternalInput").ap())
    args.append(nc.dram_tensor("out_0_dram", shape, F32, kind="ExternalOutput").ap())
    hybrid_trunk(nc, *args)
    r = _run(nc, [arrays], core_ids=[0])
    return r.results[0]["out_0_dram"]
```

```python
from contextlib import ExitStack

import concourse.bass as bass
from concourse import mybir

F32 = mybir.dt.float32
F32R = mybir.dt.float32r
ALU = mybir.AluOpType
ACT = mybir.ActivationFunctionType

P = 128
NORM_EPS = 1e-6
LN_EPS = 1e-5
GELU_CUBE = 0.044715
GELU_SCALE = 0.7978845608028654
B_ROT = 16
D_NOPE, D_ROPE, D_V = 64, 32, 64
Q_LORA, KV_LORA = 192, 128
MASKED = -3.0e38


def hybrid_trunk(nc: bass.Bass, x_in: bass.AP, g_pre_mix: bass.AP, w_in: bass.AP, a_ln_g: bass.AP,
                 a_ln_b: bass.AP, a_w_s: bass.AP, a_b_s: bass.AP, c_w_conv: bass.AP,
                 d_q_norm_g: bass.AP, d_w_uq: bass.AP, d_kv_norm_g: bass.AP, d_w_ukv: bass.AP,
                 w_branch: bass.AP, w_out: bass.AP, g_post_mix: bass.AP, g_pre_mlp: bass.AP,
                 w_mlp_in: bass.AP, w_mlp_out: bass.AP, g_post_mlp: bass.AP,
                 rope_tables: bass.AP, out: bass.AP):
    L, D, _ = w_in.shape
    S = x_in.shape[1]
    T = S // P
    KT = D // P
    MIX = w_branch.shape[2]
    FT = MIX // P
    NB = w_branch.shape[1]
    HEADS, HD = MIX // 64, 64
    FF = w_mlp_in.shape[2]
    A_GROUPS = a_w_s.shape[1]
    D_IN = Q_LORA + KV_LORA + D_ROPE
    QK = D_NOPE + D_ROPE
    assert (T, KT, FT, NB, HEADS, A_GROUPS) == (2, 8, 2, 4, 4, 4)

    COL_AV, COL_C, COL_D = MIX, 5 * MIX, 8 * MIX
    COL_GATE = COL_D + D_IN

    CHUNK = 2048
    FFC = CHUNK // KT
    STEPS = FF // FFC
    C_D, C_FEAT, C_GATE, C_BRANCH, C_OUT, C_MLP = 4, 8, 12, 28, 32, 36
    CHUNKS = C_MLP + 2 * STEPS
    C_IN2, C_LOOP = C_MLP + 2, C_MLP + 4
    RAW, RING = 4, 4
    HALVES = 2 * CHUNKS
    assert CHUNKS % RING == 0 and STEPS % 2 == 0

    CONSTS = 8

    with ExitStack() as ctx:
        def sb(name, shape, dt=F32):
            return ctx.enter_context(nc.sbuf_tensor(name, shape, dt))[:]

        def sem(name):
            return ctx.enter_context(nc.semaphore(name))

        psum = ctx.enter_context(nc.psum_tensor("banks", [P, 8, 512], F32))[:]

        raw = sb("raw", [P, RAW, CHUNK // 2])
        w_hi = sb("w_hi", [P, RING, CHUNK], F32R)
        w_lo = sb("w_lo", [P, RING, CHUNK], F32R)
        x = sb("x", [P, T, D])
        xT_hi = sb("xT_hi", [P, KT, S], F32R)
        xT_lo = sb("xT_lo", [P, KT, S], F32R)
        brT_hi = sb("brT_hi", [P, NB * FT, S], F32R)
        brT_lo = sb("brT_lo", [P, NB * FT, S], F32R)
        gain_pre = sb("gain_pre", [P, D])
        gain_post = sb("gain_post", [P, D])
        proj = sb("proj", [P, T, 4 * MIX])
        gated = proj.rearrange("p t (u n) -> p (t u) n", u=2)
        hidden_rows = proj
        rows = sb("rows", [P, T * D])
        xn = rows.rearrange("p (t d) -> p t d", t=T)
        merged = rows.rearrange("p (u n) -> p u n", u=4)
        qD = rows[:, 0:T * HEADS * QK].rearrange("p (t h e) -> p t h e", t=T, h=HEADS)
        kD = rows[:, T * HEADS * QK:2 * T * HEADS * QK].rearrange("p (t h e) -> p t h e", t=T, h=HEADS)
        rope_tmp = rows[:, 2 * T * HEADS * QK:2 * T * HEADS * QK + 512].rearrange("p (a n) -> p a n", a=4)
        hidden_sq = rows[:, 0:512]
        hidden_relu = rows[:, 512:1536].rearrange("p (b n) -> p b n", b=2)
        gate_th = sb("gate_th", [P, NB * 2 * KT * P])
        gate_v = gate_th.rearrange("p (i j n) -> p i j n", i=NB, j=4)
        th1 = gate_th[:, 2048:4096]
        th2 = gate_th[:, 4096:6144]
        th3 = gate_th[:, 6144:8192]
        d_in = th1[:, 0:T * D_IN].rearrange("p (t n) -> p t n", t=T)
        w_uq = th1[:, 704:704 + 2 * HEADS * QK].rearrange("p (k n) -> p k n", k=2)
        w_ukv = th1[:, 1472:1472 + HEADS * (D_NOPE + D_V)]
        w_s = th2[:, 0:512].rearrange("p (g s) -> p g s", g=A_GROUPS)
        w_sT = th2[:, 512:1024].rearrange("p (g t) -> p g t", g=A_GROUPS)
        ln_g = th2[:, 1024:1280]
        ln_b = th2[:, 1280:1536]
        u2 = th2[:, 1536:2048]
        z = th3[:, 0:FT * (S + 2)].rearrange("p (f n) -> p f n", f=FT)
        conv = th3[:, 516:1028].rearrange("p (f n) -> p f n", f=FT)
        u_tmp = th3[:, 1028:1540]
        a_out = u_tmp
        av2 = sb("av2", [P, T, MIX])
        av_tmp = sb("av_tmp", [P, T, MIX])
        o_sb = av_tmp
        vD = sb("vD", [P, T, HEADS * D_V])
        qTB = sb("qTB", [P, FT, S])
        kTB = sb("kTB", [P, FT, S])
        qTD = sb("qTD", [P, HEADS, S])
        kTD = sb("kTD", [P, HEADS, S])
        cqT = qTD[:, 0:2, :]
        ckvT = qTD[:, 2, :]
        probs = sb("probs", [P, 2, 3 * P])
        probsT = sb("probsT", [P, 2, 3 * P])
        bias_s = sb("bias_s", [P, FT, P])
        vec_rows = sb("vec_rows", [9, P])
        vec_cols = sb("vec_cols", [P, 9])
        tables = sb("tables", [P, T, 2 * (B_ROT // 2 + D_ROPE // 2)])
        ident = sb("ident", [P, P])
        causal = sb("causal", [P, 2 * P])
        minus_half = sb("minus_half", [P, 4])
        norm_eps = sb("norm_eps", [P, 4])
        ln_eps = sb("ln_eps", [P, T])
        ss = sb("ss", [P, 2 * T, 2])
        ms = sb("ms", [P, 2 * T, 2])
        rstd = sb("rstd", [P, 4])
        ssD = sb("ssD", [P, 2, T])
        msD = sb("msD", [P, 2, T])
        rstdD = sb("rstdD", [P, 2, T])
        ln_stats = sb("ln_stats", [P, T, 6])
        ln_mv = sb("ln_mv", [P, T, 2])
        ln_ms = sb("ln_ms", [P, T])
        ln_rstd = sb("ln_rstd", [P, T])
        neg_max = sb("neg_max", [P, 2, T])
        row_sum = sb("row_sum", [P, 2, T, HEADS])
        inv_sum = sb("inv_sum", [P, 2, T, HEADS])
        start_mark = sb("start_mark", [P, 4])

        raw_landed = [sem(f"raw_landed{s}") for s in range(RAW)]
        hi_ready = sem("hi_ready")
        lo_ready = sem("lo_ready")
        chunk_used = sem("chunk_used")
        x_landed = [sem(f"x_landed{t}") for t in range(T)]
        tables_landed = sem("tables_landed")
        gain_pre_landed = sem("gain_pre_landed")
        gain_post_landed = sem("gain_post_landed")
        side_landed = sem("side_landed")
        consts_ready = sem("consts_ready")
        x_updated = sem("x_updated")
        ss_ready = sem("ss_ready")
        ms_ready = sem("ms_ready")
        rstd_ready = sem("rstd_ready")
        xn_ready = sem("xn_ready")
        y_scaled = sem("y_scaled")
        xT_psum = sem("xT_psum")
        xT_hi_ready = sem("xT_hi_ready")
        xT_lo_ready = sem("xT_lo_ready")
        proj0_psum = sem("proj0_psum")
        proj_copied = sem("proj_copied")
        vec_psum = sem("vec_psum")
        ws_masked = sem("ws_masked")
        wsT_psum = sem("wsT_psum")
        vec_copied = sem("vec_copied")
        wsT_copied = sem("wsT_copied")
        ropeB_products = sem("ropeB_products")
        ropeB_ready = sem("ropeB_ready")
        qkTB_psum = sem("qkTB_psum")
        qkTB_copied = sem("qkTB_copied")
        av_squared = sem("av_squared")
        av_poly = sem("av_poly")
        av_inner = sem("av_inner")
        av_tanh = sem("av_tanh")
        av_gelu = sem("av_gelu")
        ln_stats_ready = sem("ln_stats_ready")
        ln_mv_ready = sem("ln_mv_ready")
        ln_ms_ready = sem("ln_ms_ready")
        ln_rstd_ready = sem("ln_rstd_ready")
        ln_centred = sem("ln_centred")
        ln_scaled = sem("ln_scaled")
        ln_ready = sem("ln_ready")
        d_in_copied = sem("d_in_copied")
        ssD_ready = sem("ssD_ready")
        msD_ready = sem("msD_ready")
        rstdD_ready = sem("rstdD_ready")
        d_normed = sem("d_normed")
        d_latentT_psum = sem("d_latentT_psum")
        d_latentT_copied = sem("d_latentT_copied")
        qD_psum = sem("qD_psum")
        kvD_psum = sem("kvD_psum")
        qkvD_copied = sem("qkvD_copied")
        ropeD_products = sem("ropeD_products")
        ropeD_ready = sem("ropeD_ready")
        qkTD_psum = sem("qkTD_psum")
        qkTD_copied = sem("qkTD_copied")
        z_ready = sem("z_ready")
        conv_tap = sem("conv_tap")
        c_out_ready = sem("c_out_ready")
        u_squared = sem("u_squared")
        u_poly = sem("u_poly")
        u_inner = sem("u_inner")
        u_tanh = sem("u_tanh")
        u_gelu = sem("u_gelu")
        sv_psum = sem("sv_psum")
        sv_biased = sem("sv_biased")
        a_out_ready = sem("a_out_ready")
        scores_psum = sem("scores_psum")
        scores_masked = sem("scores_masked")
        probs_ready = sem("probs_ready")
        probsT_psum = sem("probsT_psum")
        probsT_copied = sem("probsT_copied")
        attn_psum = sem("attn_psum")
        inv_sum_ready = sem("inv_sum_ready")
        attn_ready = sem("attn_ready")
        attnT_psum = sem("attnT_psum")
        brT_hi_ready = sem("brT_hi_ready")
        brT_lo_ready = sem("brT_lo_ready")
        gate_ready = sem("gate_ready")
        unit_psum = sem("unit_psum")
        unit_gated = sem("unit_gated")
        unit_added = sem("unit_added")
        mergedT_hi_ready = sem("mergedT_hi_ready")
        mergedT_lo_ready = sem("mergedT_lo_ready")
        y_psum = sem("y_psum")
        hidden0_psum = sem("hidden0_psum")
        hidden_copied = sem("hidden_copied")
        hiddenT_psum = sem("hiddenT_psum")
        relu_ready = sem("relu_ready")
        hidden_squared = sem("hidden_squared")
        hidden_hi_ready = sem("hidden_hi_ready")
        hidden_lo_ready = sem("hidden_lo_ready")
        stored = sem("stored")
        wait_passed = sem("wait_passed")

        SQUARES = [("x", 0, 0), ("x", 0, 1), ("y", 0, 0), ("x", 1, 0), ("y", 0, 1), ("x", 1, 1),
                   ("y", 1, 0), ("y", 1, 1)]
        ORDER_C, ORDER_A, ORDER_B, ORDER_D = range(4)

        w_in_v = w_in.rearrange("l (k p) c -> l p k c", p=P)
        w_br_v = w_branch.rearrange("l i (k p) n -> l i p k n", p=P)
        w_out_v = w_out.rearrange("l (c k p) n -> l c p k n", p=P, k=2)
        mlp_in_v = w_mlp_in.rearrange("l (k p) (j c) -> l j p k c", p=P, c=FFC)
        mlp_out_v = w_mlp_out.rearrange("l (j k p) n -> l j p k n", p=P, k=FFC // P)
        PAIRS = STEPS // 2 - 2
        mlp_in_loop = w_mlp_in[:, :, 3 * FFC:FF - FFC].rearrange(
            "l (k p) (i b c) -> l i b p k c", p=P, b=2, c=FFC)
        mlp_out_loop = w_mlp_out[:, FFC:FF - 3 * FFC, :].rearrange(
            "l (i b k p) n -> l i b p k n", p=P, b=2, k=FFC // P)
        x_v = x_in.rearrange("a (t p) d -> t p (a d)", p=P)
        out_v = out.rearrange("a (t p) d -> t p (a d)", p=P)

        def shape_of(c):
            if c < C_D:
                return 4, 512
            if c < C_FEAT:
                return 2, D_IN
            if c < C_BRANCH:
                return KT, 256
            if c < C_MLP:
                return 2, D
            return (KT, FFC) if c < C_IN2 or (c % 2 == 0 and c < CHUNKS - 3) else (2, D)

        def size_of(c):
            k, n = shape_of(c)
            return k * n

        def view(buf, c):
            k, n = shape_of(c)
            return buf[:, c % RING, 0:k * n].rearrange("p (k n) -> p k n", k=k)

        def both(c):
            return view(w_hi, c), view(w_lo, c)

        def nth(l, per_layer, i):
            return l * per_layer + i + 1

        def used(l, c):
            return nth(l, CHUNKS, c) + RING

        def split_done(l, c):
            return nth(l, HALVES, 2 * c + 1) + 2 * RING

        def row_half(k, t, h):
            return 4 * k + 2 * t + h

        def columns(h):
            return slice(h * (D // 2), (h + 1) * (D // 2))

        def apart(eng):
            eng.sem_inc(wait_passed, 1)

        block = ctx.enter_context(nc.Block())

        @block.sync
        def _(sp):
            def load(l, c, src, i=0):
                k, n = shape_of(c)
                for h in range(2):
                    q = 2 * c + h
                    sp.wait_ge(lo_ready, nth(l, HALVES, q + 8 * i) + 2 * RING - RAW)
                    if c == C_GATE - 1:
                        apart(sp)
                    dst = raw[:, q % RAW, 0:k * n // 2].rearrange("p (k n) -> p k n", k=k // 2)
                    sp.dma_start(dst, src[:, h * k // 2:(h + 1) * k // 2, :]).then_inc(raw_landed[q % RAW], 16)

            for t in range(T):
                sp.dma_start(x[:, t, :], x_v[t]).then_inc(x_landed[t], 16)
            with sp.Fori(0, L) as l:
                sp.dma_start(gain_pre, g_pre_mix[l].partition_broadcast(P)).then_inc(gain_pre_landed, 16)
                for c in range(C_D):
                    g, kh = c // 2, c % 2
                    col = COL_AV + 512 * g
                    load(l, c, w_in_v[l, :, 4 * kh:4 * kh + 4, col:col + 512])
                side = [
                    (vec_rows[0:6, :], c_w_conv[l].rearrange("k (f p) -> (k f) p", p=P)),
                    (vec_rows[6:7, :], d_q_norm_g[l, 0:P].unsqueeze(0)),
                    (vec_rows[7:8, 0:Q_LORA - P], d_q_norm_g[l, P:Q_LORA].unsqueeze(0)),
                    (vec_rows[8:9, :], d_kv_norm_g[l].unsqueeze(0)),
                    (w_s, a_w_s[l].rearrange("g t s -> t g s")),
                    (ln_g, a_ln_g[l].partition_broadcast(P)),
                    (ln_b, a_ln_b[l].partition_broadcast(P)),
                    (w_uq[:, 0, :], d_w_uq[l, 0:P].rearrange("r h e -> r (h e)")),
                    (w_uq[0:Q_LORA - P, 1, :], d_w_uq[l, P:Q_LORA].rearrange("r h e -> r (h e)")),
                    (w_ukv, d_w_ukv[l].rearrange("r h e -> r (h e)")),
                ]
                for g in range(A_GROUPS):
                    half = 64 * (g % 2)
                    side.append((bias_s[half:half + 64, g // 2, :], a_b_s[l, g].partition_broadcast(64)))
                for dst, src in side:
                    sp.dma_start(dst, src).then_inc(side_landed, 16)
                for c in range(C_D, C_FEAT):
                    k0 = 2 * (c - C_D)
                    load(l, c, w_in_v[l, :, k0:k0 + 2, COL_D:COL_D + D_IN])
                for c in range(C_FEAT, C_GATE):
                    col = COL_C + 256 * (c - C_FEAT) if c < C_GATE - 1 else 0
                    load(l, c, w_in_v[l, :, :, col:col + 256])
                sp.wait_ge(xn_ready, nth(l, 8, row_half(0, 1, 1)))
                sp.dma_start(gain_pre, g_pre_mlp[l].partition_broadcast(P)).then_inc(gain_pre_landed, 16)
                sp.dma_start(gain_post, g_post_mix[l].partition_broadcast(P)).then_inc(gain_post_landed, 16)
                for c in range(C_GATE, C_BRANCH):
                    col = COL_GATE + 256 * (c - C_GATE)
                    load(l, c, w_in_v[l, :, :, col:col + 256])
                for c in range(C_BRANCH, C_OUT):
                    load(l, c, w_br_v[l, c - C_BRANCH])
                for c in range(C_OUT, C_MLP):
                    load(l, c, w_out_v[l, c - C_OUT])
                load(l, C_MLP, mlp_in_v[l, 0])
                load(l, C_MLP + 1, mlp_in_v[l, 1])
                load(l, C_IN2, mlp_in_v[l, 2])
                load(l, C_LOOP - 1, mlp_out_v[l, 0])
                with sp.Fori(0, PAIRS) as i:
                    for b in range(2):
                        c = C_LOOP + 2 * b
                        load(l, c, mlp_in_loop[l, i, b], i)
                        load(l, c + 1, mlp_out_loop[l, i, b], i)
                load(l, CHUNKS - 4, mlp_in_v[l, STEPS - 1])
                for k in range(STEPS - 3, STEPS):
                    load(l, CHUNKS - STEPS + k, mlp_out_v[l, k])
                sp.wait_ge(y_scaled, nth(l, 8, row_half(0, 1, 1)))
                sp.dma_start(gain_post, g_post_mlp[l].partition_broadcast(P)).then_inc(gain_post_landed, 16)
            for t in range(T):
                sp.wait_ge(x_updated, 8 + nth(L - 1, 8, row_half(1, t, 1)))
                sp.dma_start(out_v[t], x[:, t, :]).then_inc(stored, 16)
            sp.wait_ge(stored, 16 * T)

        @block.scalar
        def _(act):
            def split_half(l, c, h, i=0):
                q = 2 * c + h
                act.wait_ge(raw_landed[q % RAW], 16 * (l * (HALVES // RAW) + i * (8 // RAW) + q // RAW + 1))
                if h == 0:
                    act.wait_ge(chunk_used, nth(l, CHUNKS, c + 4 * i))
                n = size_of(c) // 2
                nc.scalar.copy(w_hi[:, c % RING, h * n:(h + 1) * n], raw[:, q % RAW, 0:n]).then_inc(hi_ready, 1)

            def split(l, c, i=0):
                for h in range(2):
                    split_half(l, c, h, i)

            def x_squares(l, k, t):
                for h in range(2):
                    act.wait_ge(x_updated, nth(l, 8, row_half(0, t, h)) + (4 if k == 0 else 8))
                    nc.scalar.activation(xn[:, t, columns(h)], x[:, t, columns(h)], ACT.Square,
                                         scale=float(D) ** -0.5, accum_out=ss[:, t, h:h + 1]
                                         ).then_inc(ss_ready, 1)

            def y_square(l, k, t, h):
                if t == T - 1 and h == 1:
                    act.wait_ge(chunk_used, used(l, (C_MLP if k == 0 else CHUNKS) - 1))
                else:
                    act.wait_ge(y_psum, nth(l, 6, 3 * k + 2 * t + h))
                nc.scalar.activation(xn[:, t, columns(h)], psum[:, 2 * t + h, :], ACT.Square,
                                     scale=float(D) ** -0.5, accum_out=ss[:, T + t, h:h + 1]
                                     ).then_inc(ss_ready, 1)

            def xT_evacuate(l, k, t):
                for b in range(2):
                    act.wait_ge(xT_psum, nth(l, 8, row_half(k, t, b)))
                    nc.scalar.copy(xT_hi[:, 4 * b:4 * b + 4, t * P:(t + 1) * P],
                                   psum[:, 4 + 2 * t + b, :].rearrange("p (k n) -> p k n", k=4)
                                   ).then_inc(xT_hi_ready, 1)

            def gate_tanh(l, g):
                act.wait_ge(chunk_used, used(l, C_GATE + g))
                nc.scalar.activation(gate_v[:, g // 4, g % 4, :], psum[:, 6 + g % 2, :], ACT.Tanh,
                                     scale=0.5).then_inc(gate_ready, 1)

            def head_exp(l, h):
                for t in range(T):
                    act.wait_ge(scores_masked, nth(l, 16, 2 * h + t))
                    part = probs[:, h % 2, 0:P] if t == 0 else probs[:, h % 2, P:3 * P]
                    nc.scalar.activation(part, part, ACT.Exp, bias=neg_max[:, h % 2, t:t + 1], scale=-1.0,
                                         accum_out=row_sum[:, h // 4, t, h % 4:h % 4 + 1]).then_inc(probs_ready, 1)

            def head_copy(l, h):
                act.wait_ge(probsT_psum, nth(l, 8, h))
                nc.scalar.copy(probsT[:, h % 2, :], psum[:, 2, 0:3 * P]).then_inc(probsT_copied, 1)

            def branch_hi(l, i, src):
                nc.scalar.copy(brT_hi[:, FT * i:FT * i + FT, :].rearrange("p f n -> p (f n)"), src
                               ).then_inc(brT_hi_ready, 1)

            def side_step(l, s):
                if s == 4:
                    act.wait_ge(vec_psum, nth(l, 1, 0))
                    nc.scalar.copy(vec_cols, psum[:, 6, 0:9]).then_inc(vec_copied, 1)
                    act.wait_ge(wsT_psum, nth(l, 1, 0))
                    nc.scalar.copy(w_sT.rearrange("p g t -> p (g t)"), psum[:, 7, :]).then_inc(wsT_copied, 1)
                    act.wait_ge(proj_copied, nth(l, 4, 3))
                    nc.scalar.activation(av_tmp, proj[:, :, 0:MIX], ACT.Square).then_inc(av_squared, 1)
                if s == 5:
                    act.wait_ge(av_inner, nth(l, 1, 0))
                    nc.scalar.activation(av_tmp, av_tmp, ACT.Tanh, scale=GELU_SCALE).then_inc(av_tanh, 1)
                if s == 6:
                    for n, dst in enumerate((qTB, kTB)):
                        act.wait_ge(qkTB_psum, nth(l, 2, n))
                        nc.scalar.copy(dst.rearrange("p f n -> p (f n)"), psum[:, 6 + n, :]).then_inc(qkTB_copied, 1)
                if s == 8:
                    act.wait_ge(chunk_used, used(l, C_FEAT - 1))
                    for t in range(T):
                        nc.scalar.copy(d_in[:, t, :], psum[:, 4 + t, 0:D_IN]).then_inc(d_in_copied, 1)
                    act.wait_ge(d_in_copied, nth(l, 2, 1))
                    for t in range(T):
                        for n, (a, b) in enumerate(((0, Q_LORA), (Q_LORA, Q_LORA + KV_LORA))):
                            nc.scalar.activation(psum[:, 4 + t, a:b], psum[:, 4 + t, a:b], ACT.Square,
                                                 scale=float(b - a) ** -0.5, accum_out=ssD[:, n, t:t + 1]).then_inc(ssD_ready, 1)
                if s == 10:
                    act.wait_ge(d_latentT_psum, nth(l, 1, 0))
                    act.wait_ge(vec_copied, nth(l, 1, 0))
                    nc.scalar.activation(cqT[:, 0, :], psum[:, 4, 0:S], ACT.Copy, scale=vec_cols[:, 6:7])
                    nc.scalar.activation(ckvT, psum[:, 4, S:2 * S], ACT.Copy, scale=vec_cols[:, 8:9])
                    nc.scalar.activation(cqT[0:Q_LORA - P, 1, :], psum[0:Q_LORA - P, 5, 0:S], ACT.Copy,
                                         scale=vec_cols[0:Q_LORA - P, 7:8]).then_inc(d_latentT_copied, 1)
                if s == 11:
                    for t in range(T):
                        act.wait_ge(qD_psum, nth(l, 2, t))
                        nc.scalar.copy(qD[:, t].rearrange("p h e -> p (h e)"), psum[:, 4 + t, 0:HEADS * QK])
                    for t in range(T):
                        act.wait_ge(kvD_psum, nth(l, 2, t))
                        kv = psum[:, 6 + t, :].rearrange("p (h e) -> p h e", h=HEADS)
                        nc.scalar.copy(kD[:, t, :, 0:D_NOPE], kv[:, :, 0:D_NOPE])
                        last = nc.scalar.copy(vD[:, t, :].rearrange("p (h e) -> p h e", h=HEADS),
                                              kv[:, :, D_NOPE:D_NOPE + D_V])
                    last.then_inc(qkvD_copied, 1)
                if s == 12:
                    act.wait_ge(chunk_used, used(l, C_GATE - 1))
                    nc.scalar.activation(u_tmp, psum[:, 3, :], ACT.Square).then_inc(u_squared, 1)
                if s == 13:
                    act.wait_ge(u_inner, nth(l, 1, 0))
                    nc.scalar.activation(u_tmp, u_tmp, ACT.Tanh, scale=GELU_SCALE).then_inc(u_tanh, 1)
                if s in (13, 14):
                    for n in range(2):
                        j = 2 * (s - 13) + n
                        act.wait_ge(qkTD_psum, nth(l, 4, j))
                        dst = (qTD, kTD)[j // 2][0:QK, 2 * (j % 2):2 * (j % 2) + 2, :]
                        nc.scalar.copy(dst, psum[0:QK, 4 + n, :].rearrange("p (h n) -> p h n", h=2)
                                       ).then_inc(qkTD_copied, 1)
                if s == 14:
                    act.wait_ge(c_out_ready, nth(l, 1, 0))
                    branch_hi(l, 2, conv.rearrange("p f n -> p (f n)"))
                if 15 <= s < 23:
                    head_copy(l, s - 15)
                if 14 <= s < 22:
                    head_exp(l, s - 14)
                if s == 16:
                    act.wait_ge(a_out_ready, nth(l, 1, 0))
                    branch_hi(l, 0, a_out)
                if s in (20, 24):
                    n = (s - 20) // 4
                    act.wait_ge(attnT_psum, nth(l, 2, n))
                    branch_hi(l, (1, 3)[n], psum[:, 4, :])
                if C_GATE < s <= C_BRANCH:
                    gate_tanh(l, s - C_GATE - 1)

            with act.Fori(0, L) as l:
                for t in range(T):
                    x_squares(l, 0, t)
                split(l, 0)
                xT_evacuate(l, 0, 0)
                split(l, 1)
                split(l, 2)
                xT_evacuate(l, 0, 1)
                split(l, 3)
                for g in range(2):
                    for t in range(T):
                        if t == 0:
                            act.wait_ge(proj0_psum, nth(l, 2, g))
                        else:
                            act.wait_ge(chunk_used, used(l, 2 * g + 1))
                        nc.scalar.copy(proj[:, t, 512 * g:512 * g + 512], psum[:, 2 * t + g, :]
                                       ).then_inc(proj_copied, 1)
                    split(l, 4 + 2 * g)
                    if g == 0:
                        split(l, 5)
                for s in range(4, C_OUT):
                    if s == 5:
                        split(l, s + 3)
                        side_step(l, s)
                    else:
                        side_step(l, s)
                        split(l, s + 3)
                for u in range(4):
                    act.wait_ge(unit_added, nth(l, 12, 8 + u))
                    nc.scalar.activation(xT_hi[:, 2 * u:2 * u + 2, :].rearrange("p k n -> p (k n)"),
                                         merged[:, u, :], ACT.Copy, scale=0.5).then_inc(mergedT_hi_ready, 1)
                split(l, C_OUT + 3)
                y_square(l, 0, 0, 0)
                y_square(l, 0, 0, 1)
                split_half(l, C_MLP, 0)
                x_squares(l, 1, 0)
                split_half(l, C_MLP, 1)
                split(l, C_MLP + 1)
                xT_evacuate(l, 1, 0)
                y_square(l, 0, 1, 0)
                y_square(l, 0, 1, 1)
                split_half(l, C_IN2, 0)
                x_squares(l, 1, 1)
                split_half(l, C_IN2, 1)

                def hidden_copy(t):
                    if t == 0:
                        act.wait_ge(hidden0_psum, nth(l, 1, 0))
                    else:
                        act.wait_ge(chunk_used, used(l, C_MLP + 1))
                    nc.scalar.copy(hidden_rows[:, t, 0:2 * FFC], psum[:, 2 * t, :]).then_inc(hidden_copied, 1)

                hidden_copy(0)
                xT_evacuate(l, 1, 1)
                split(l, C_IN2 + 1)
                split(l, C_LOOP)
                hidden_copy(1)

                def hidden_hi(k, i=0):
                    if k < 2:
                        act.wait_ge(hiddenT_psum, nth(l, 2, k))
                        bank = 1 + 2 * k
                    else:
                        act.wait_ge(chunk_used, used(l, C_MLP + 2 * k - 1 + 4 * i))
                        bank = 4 + k % 2
                    nc.scalar.activation(hidden_relu[:, k % 2, :], psum[:, bank, :], ACT.Relu
                                         ).then_inc(relu_ready, 1)
                    act.wait_ge(relu_ready, nth(l, STEPS, k + 2 * i))
                    nc.scalar.activation(brT_hi[:, 2 * (k % 2):2 * (k % 2) + 2, :].rearrange("p f n -> p (f n)"),
                                         hidden_relu[:, k % 2, :], ACT.Square).then_inc(hidden_hi_ready, 1)

                hidden_hi(0)
                hidden_hi(1)
                split(l, C_LOOP + 1)
                with act.Fori(0, PAIRS) as i:
                    for b in range(2):
                        c = C_LOOP + 2 * b
                        split(l, c + 2, i)
                        hidden_hi(2 + b, i)
                        split(l, c + 3, i)
                split(l, CHUNKS - 2)
                hidden_hi(STEPS - 2)
                split(l, CHUNKS - 1)
                hidden_hi(STEPS - 1)
                for t in range(T):
                    for h in range(2):
                        y_square(l, 1, t, h)

        @block.vector
        def _(dve):
            v = nc.vector

            def split_half(l, c, h, i=0):
                q = 2 * c + h
                dve.wait_ge(hi_ready, nth(l, HALVES, q + 8 * i))
                n = size_of(c) // 2
                cut = slice(h * n, (h + 1) * n)
                v.tensor_tensor(w_lo[:, c % RING, cut], raw[:, q % RAW, 0:n],
                                w_hi[:, c % RING, cut].bitcast(F32), ALU.subtract).then_inc(lo_ready, 1)

            def split(l, c, i=0):
                for h in range(2):
                    split_half(l, c, h, i)

            def normalise(l, k, t):
                dve.wait_ge(gain_pre_landed, 16 * nth(l, 2, k))
                dve.wait_ge(rstd_ready, nth(l, 8, (0, 1, 3, 5)[2 * k + t]))
                for h in range(2):
                    v.scalar_tensor_tensor(xn[:, t, columns(h)], x[:, t, columns(h)], rstd[:, t:t + 1],
                                           gain_pre[:, columns(h)], ALU.mult, ALU.mult).then_inc(xn_ready, 1)

            def xT_evacuate(l, k, t):
                for b in range(2):
                    dve.wait_ge(xT_hi_ready, nth(l, 8, row_half(k, t, b)))
                    cut = slice(t * P, (t + 1) * P)
                    v.tensor_tensor(xT_lo[:, 4 * b:4 * b + 4, cut],
                                    psum[:, 4 + 2 * t + b, :].rearrange("p (k n) -> p k n", k=4),
                                    xT_hi[:, 4 * b:4 * b + 4, cut].bitcast(F32), ALU.subtract
                                    ).then_inc(xT_lo_ready, 1)

            def scale_y(l, k, t, h):
                dve.wait_ge(gain_post_landed, 16 * nth(l, 2, k))
                dve.wait_ge(ss_ready, nth(l, 16, SQUARES.index(("y", k, t)) * 2 + h))
                v.tensor_tensor(xn[:, t, columns(h)], psum[:, 2 * t + h, :], gain_post[:, columns(h)], ALU.mult
                                ).then_inc(y_scaled, 1)

            def residual(l, k, t):
                dve.wait_ge(rstd_ready, nth(l, 8, (2, 4, 6, 7)[2 * k + t]))
                for h in range(2):
                    dve.wait_ge(y_scaled, nth(l, 8, row_half(k, t, h)))
                    v.scalar_tensor_tensor(x[:, t, columns(h)], xn[:, t, columns(h)], rstd[:, T + t:T + t + 1],
                                           x[:, t, columns(h)], ALU.mult, ALU.add).then_inc(x_updated, 1)

            def rope(l, x1, x2, cos, sin, shape, products, n, per_layer):
                size = 1
                for d in shape[1:]:
                    size *= d
                names = "abcd"[:len(shape) - 1]
                sizes = {names[i]: shape[i + 1] for i in range(len(names) - 1)}
                tmp = [rope_tmp[:, i, 0:size].rearrange(f"p ({' '.join(names)}) -> p {' '.join(names)}", **sizes)
                       for i in range(4)]
                v.tensor_tensor(tmp[0], x1, cos, ALU.mult)
                v.tensor_tensor(tmp[1], x2, sin, ALU.mult)
                v.tensor_tensor(tmp[2], x2, cos, ALU.mult)
                v.tensor_tensor(tmp[3], x1, sin, ALU.mult).then_inc(products, 1)
                dve.wait_ge(products, nth(l, per_layer, n))
                return tmp

            def table(offset, half, shape):
                t = tables[:, :, offset:offset + half]
                return t.unsqueeze(2).broadcast_to(shape) if len(shape) == 4 else t

            def head_mask(l, h):
                scale = -(float(HD) ** -0.5 if h < 4 else float(QK) ** -0.5)
                dve.wait_ge(scores_psum, nth(l, 8, h))
                bank = psum[:, h % 2, :]
                apart(dve)
                v.tensor_tensor_reduce(probs[:, h % 2, 0:P], bank[:, 0:P], causal[:, P:2 * P], scale, 3.0e38,
                                       ALU.add, ALU.min, neg_max[:, h % 2, 0:1]).then_inc(scores_masked, 1)
                v.tensor_tensor_reduce(probs[:, h % 2, P:3 * P], bank[:, P:3 * P], causal, scale, 3.0e38,
                                       ALU.add, ALU.min, neg_max[:, h % 2, 1:2]).then_inc(scores_masked, 1)

            def branch_lo(l, i, order, src):
                dve.wait_ge(brT_hi_ready, nth(l, 4, order))
                flat = "p f n -> p (f n)"
                v.tensor_tensor(brT_lo[:, FT * i:FT * i + FT, :].rearrange(flat), src,
                                brT_hi[:, FT * i:FT * i + FT, :].rearrange(flat).bitcast(F32), ALU.subtract
                                ).then_inc(brT_lo_ready, 1)

            def side_step(l, s):
                if s == 4:
                    dve.wait_ge(proj_copied, nth(l, 4, 3))
                    qk = proj[:, :, MIX:3 * MIX].rearrange("p t (h e) -> p t h e", e=HD)
                    h = B_ROT // 2
                    shape = [P, T, 2 * HEADS, h]
                    x1, x2 = qk[:, :, :, 0:h], qk[:, :, :, h:2 * h]
                    tmp = rope(l, x1, x2, table(0, h, shape), table(h, h, shape), shape,
                               ropeB_products, 0, 1)
                    v.tensor_tensor(x1, tmp[0], tmp[1], ALU.subtract)
                    v.tensor_tensor(x2, tmp[2], tmp[3], ALU.add).then_inc(ropeB_ready, 1)
                if s == 5:
                    dve.wait_ge(av_squared, nth(l, 1, 0))
                    v.tensor_scalar(av2, av_tmp, GELU_CUBE, 1.0, ALU.mult, ALU.add).then_inc(av_poly, 1)
                    dve.wait_ge(av_poly, nth(l, 1, 0))
                    v.tensor_tensor(av_tmp, av2, proj[:, :, 0:MIX], ALU.mult).then_inc(av_inner, 1)
                if s == 6:
                    dve.wait_ge(av_tanh, nth(l, 1, 0))
                    v.scalar_tensor_tensor(av2, av_tmp, 1.0, proj[:, :, 0:MIX], ALU.add, ALU.mult
                                           ).then_inc(av_gelu, 1)
                    dve.wait_ge(av_gelu, nth(l, 1, 0))
                    for t in range(T):
                        v.bn_stats(ln_stats[:, t, :], av2[:, t, :]).then_inc(ln_stats_ready, 1)
                    dve.wait_ge(ln_stats_ready, nth(l, 2, 1))
                    apart(dve)
                    for t in range(T):
                        v.bn_aggr(ln_mv[:, t, :], ln_stats[:, t, :]).then_inc(ln_mv_ready, 1)
                if s == 7:
                    dve.wait_ge(ln_rstd_ready, nth(l, 1, 0))
                    for t in range(T):
                        v.tensor_scalar(av2[:, t, :], av2[:, t, :], ln_mv[:, t, 0:1], ln_rstd[:, t:t + 1],
                                        ALU.subtract, ALU.mult).then_inc(ln_centred, 1)
                    dve.wait_ge(ln_centred, nth(l, 2, 1))
                    dve.wait_ge(side_landed, 16 * nth(l, 14, 13))
                    wide = [P, T, MIX]
                    v.tensor_tensor(av2, av2, ln_g.unsqueeze(1).broadcast_to(wide), ALU.mult).then_inc(ln_scaled, 1)
                    dve.wait_ge(ln_scaled, nth(l, 1, 0))
                    v.tensor_tensor(av2, av2, ln_b.unsqueeze(1).broadcast_to(wide), ALU.add).then_inc(ln_ready, 1)
                if s == 8:
                    dve.wait_ge(rstdD_ready, nth(l, 1, 0))
                    for t in range(T):
                        for n, (a, b) in enumerate(((0, Q_LORA), (Q_LORA, Q_LORA + KV_LORA))):
                            last = v.tensor_scalar(d_in[:, t, a:b], d_in[:, t, a:b], rstdD[:, n, t:t + 1], None,
                                                   ALU.mult)
                    last.then_inc(d_normed, 1)
                if s == 11:
                    dve.wait_ge(chunk_used, used(l, C_FEAT + 2))
                    banks = [psum[:, b, :].rearrange("p (f n) -> p f n", f=FT) for b in range(3)]
                    v.memset(z[:, :, 0:2], 0.0)
                    v.tensor_copy(conv, banks[1]).then_inc(z_ready, 1)
                    dve.wait_ge(z_ready, nth(l, 2, 0))
                    v.tensor_tensor(z[:, :, 2:S + 2], conv, banks[2], ALU.mult).then_inc(z_ready, 1)
                    dve.wait_ge(z_ready, nth(l, 2, 1))
                    dve.wait_ge(vec_copied, nth(l, 1, 0))
                    for f in range(FT):
                        last = v.tensor_scalar(conv[:, f, :], z[:, f, 2:S + 2], vec_cols[:, 4 + f:5 + f], None,
                                               ALU.mult)
                    last.then_inc(conv_tap, 1)
                    for k in (1, 0):
                        dve.wait_ge(conv_tap, nth(l, 3, 1 - k))
                        for f in range(FT):
                            last = v.scalar_tensor_tensor(conv[:, f, :], z[:, f, k:S + k],
                                                          vec_cols[:, 2 * k + f:2 * k + f + 1], conv[:, f, :],
                                                          ALU.mult, ALU.add)
                        last.then_inc(conv_tap, 1)
                    dve.wait_ge(conv_tap, nth(l, 3, 2))
                    v.tensor_tensor(conv, conv, banks[0], ALU.mult).then_inc(c_out_ready, 1)
                if s == 12:
                    dve.wait_ge(qkvD_copied, nth(l, 1, 0))
                    h, o = D_ROPE // 2, B_ROT
                    shape = [P, T, HEADS, h]
                    x1, x2 = qD[:, :, :, D_NOPE:D_NOPE + h], qD[:, :, :, D_NOPE + h:QK]
                    tmp = rope(l, x1, x2, table(o, h, shape), table(o + h, h, shape), shape,
                               ropeD_products, 0, 2)
                    v.tensor_tensor(x1, tmp[0], tmp[1], ALU.subtract)
                    v.tensor_tensor(x2, tmp[2], tmp[3], ALU.add).then_inc(ropeD_ready, 1)
                    dve.wait_ge(ropeD_ready, nth(l, 2, 0))
                    kr = d_in[:, :, Q_LORA + KV_LORA:D_IN]
                    tmp = rope(l, kr[:, :, 0:h], kr[:, :, h:D_ROPE], table(o, h, [P, T, h]),
                               table(o + h, h, [P, T, h]), [P, T, h], ropeD_products, 1, 2)
                    tmp = [a.unsqueeze(2).broadcast_to(shape) for a in tmp]
                    v.tensor_tensor(kD[:, :, :, D_NOPE:D_NOPE + h], tmp[0], tmp[1], ALU.subtract)
                    v.tensor_tensor(kD[:, :, :, D_NOPE + h:QK], tmp[2], tmp[3], ALU.add).then_inc(ropeD_ready, 1)
                    dve.wait_ge(u_squared, nth(l, 1, 0))
                    v.tensor_scalar(u2, u_tmp, GELU_CUBE, 1.0, ALU.mult, ALU.add).then_inc(u_poly, 1)
                    dve.wait_ge(u_poly, nth(l, 1, 0))
                    v.tensor_tensor(u_tmp, u2, psum[:, 3, :], ALU.mult).then_inc(u_inner, 1)
                if s == 13:
                    dve.wait_ge(u_tanh, nth(l, 1, 0))
                    v.scalar_tensor_tensor(u2, u_tmp, 1.0, psum[:, 3, :], ALU.add, ALU.mult).then_inc(u_gelu, 1)
                if s == 14:
                    branch_lo(l, 2, ORDER_C, conv.rearrange("p f n -> p (f n)"))
                if 14 <= s < 22:
                    head_mask(l, s - 14)
                if s == 15:
                    dve.wait_ge(sv_psum, nth(l, 1, 0))
                    dve.wait_ge(u_gelu, nth(l, 1, 0))
                    four = [P, FT, T, P]
                    sv = psum[:, 4, :].rearrange("p (f t n) -> p f t n", f=FT, t=T)
                    v.tensor_tensor(a_out.rearrange("p (f t n) -> p f t n", f=FT, t=T), sv,
                                    bias_s.unsqueeze(2).broadcast_to(four), ALU.add).then_inc(sv_biased, 1)
                    dve.wait_ge(sv_biased, nth(l, 1, 0))
                    v.scalar_tensor_tensor(a_out, u2, 0.5, a_out, ALU.mult, ALU.mult).then_inc(a_out_ready, 1)
                if s == 16:
                    branch_lo(l, 0, ORDER_A, a_out)
                if s in (19, 23):
                    n = (s - 19) // 4
                    dve.wait_ge(probs_ready, nth(l, 16, 8 * n + 7))
                    v.reciprocal(inv_sum[:, n], row_sum[:, n]).then_inc(inv_sum_ready, 1)
                    dve.wait_ge(inv_sum_ready, nth(l, 2, n))
                    dve.wait_ge(attn_psum, nth(l, 8, 4 * n + 3))
                    four = [P, T, HEADS, HD]
                    bank = psum[:, (3, 5)[n], :].rearrange("p (t h e) -> p t h e", t=T, h=HEADS)
                    v.tensor_tensor(o_sb.rearrange("p t (h e) -> p t h e", h=HEADS), bank,
                                    inv_sum[:, n].unsqueeze(3).broadcast_to(four), ALU.mult
                                    ).then_inc(attn_ready, 1)
                if s in (20, 24):
                    n = (s - 20) // 4
                    branch_lo(l, (1, 3)[n], (ORDER_B, ORDER_D)[n], psum[:, 4, :])
                if C_BRANCH < s <= C_OUT:
                    gate_units(l, s - C_BRANCH - 1)

            def gate_units(l, i):
                for u in range(4):
                    if u < 3:
                        dve.wait_ge(unit_psum, nth(l, 12, 3 * i + u))
                    else:
                        dve.wait_ge(chunk_used, used(l, C_BRANCH + i))
                    if i == 0:
                        dve.wait_ge(gate_ready, nth(l, 16, 15))
                    if i >= 2:
                        dve.wait_ge(unit_added, nth(l, 12, 4 * (i - 2) + u))
                    dst = merged[:, u, :] if i == 0 else gated[:, u, :]
                    v.scalar_tensor_tensor(dst, gate_v[:, i, u, :], 1.0, psum[:, 4 + u, :], ALU.add, ALU.mult
                                           ).then_inc(unit_gated, 1)

            v.memset(start_mark[:, 0:1], 0.0).then_inc(lo_ready, 2 * RING)
            v.memset(start_mark[:, 1:2], 0.0).then_inc(chunk_used, RING)
            for t in range(T):
                dve.wait_ge(x_landed[t], 16)
                v.memset(start_mark[:, 2 + t:3 + t], 0.0).then_inc(x_updated, 6 if t == 0 else 2)
            with dve.Fori(0, L) as l:
                normalise(l, 0, 0)
                normalise(l, 0, 1)
                split(l, 0)
                xT_evacuate(l, 0, 0)
                split(l, 1)
                split(l, 2)
                xT_evacuate(l, 0, 1)
                for c in range(3, 7):
                    split(l, c)
                dve.wait_ge(tables_landed, 16)
                for s in range(4, C_OUT):
                    side_step(l, s)
                    split(l, s + 3)
                side_step(l, C_OUT)
                for u in range(4):
                    dve.wait_ge(mergedT_hi_ready, nth(l, 4, u))
                    flat = "p k n -> p (k n)"
                    v.scalar_tensor_tensor(xT_lo[:, 2 * u:2 * u + 2, :].rearrange(flat), merged[:, u, :], 0.5,
                                           xT_hi[:, 2 * u:2 * u + 2, :].rearrange(flat).bitcast(F32),
                                           ALU.mult, ALU.subtract).then_inc(mergedT_lo_ready, 1)
                split(l, C_OUT + 3)
                scale_y(l, 0, 0, 0)
                scale_y(l, 0, 0, 1)
                residual(l, 0, 0)
                split_half(l, C_MLP, 0)
                normalise(l, 1, 0)
                split_half(l, C_MLP, 1)
                split_half(l, C_MLP + 1, 0)
                xT_evacuate(l, 1, 0)
                split_half(l, C_MLP + 1, 1)
                scale_y(l, 0, 1, 0)
                scale_y(l, 0, 1, 1)
                residual(l, 0, 1)
                split_half(l, C_IN2, 0)
                normalise(l, 1, 1)
                xT_evacuate(l, 1, 1)
                split_half(l, C_IN2, 1)
                split(l, C_IN2 + 1)
                split(l, C_LOOP)

                def hidden(k, i=0):
                    if k >= 1:
                        dve.wait_ge(hidden_lo_ready, nth(l, STEPS, k - 1 + 2 * i))
                    dve.wait_ge(relu_ready, nth(l, STEPS, k + 2 * i))
                    v.tensor_tensor(hidden_sq, hidden_relu[:, k % 2, :], hidden_relu[:, k % 2, :], ALU.mult
                                    ).then_inc(hidden_squared, 1)
                    dve.wait_ge(hidden_squared, nth(l, STEPS, k + 2 * i))
                    dve.wait_ge(hidden_hi_ready, nth(l, STEPS, k + 2 * i))
                    flat = "p f n -> p (f n)"
                    half = slice(2 * (k % 2), 2 * (k % 2) + 2)
                    v.tensor_tensor(brT_lo[:, half, :].rearrange(flat), hidden_sq,
                                    brT_hi[:, half, :].rearrange(flat).bitcast(F32), ALU.subtract
                                    ).then_inc(hidden_lo_ready, 1)

                hidden(0)
                hidden(1)
                split(l, C_LOOP + 1)
                with dve.Fori(0, PAIRS) as i:
                    for b in range(2):
                        c = C_LOOP + 2 * b
                        split(l, c + 2, i)
                        hidden(2 + b, i)
                        split(l, c + 3, i)
                split(l, CHUNKS - 2)
                hidden(STEPS - 2)
                split(l, CHUNKS - 1)
                hidden(STEPS - 1)
                for t in range(T):
                    scale_y(l, 1, t, 0)
                    scale_y(l, 1, t, 1)
                    residual(l, 1, t)

        @block.gpsimd
        def _(pool):
            g = nc.gpsimd
            sp_tables = rope_tables.rearrange("(t p) n -> p t n", p=P)
            pool.dma_start(tables, sp_tables).then_inc(tables_landed, 16)
            g.memset(ident, 0.0).then_inc(consts_ready, 1)
            g.memset(causal, 0.0).then_inc(consts_ready, 1)
            g.memset(minus_half, -0.5).then_inc(consts_ready, 1)
            g.memset(vec_rows, 0.0).then_inc(consts_ready, 1)
            g.memset(norm_eps, NORM_EPS).then_inc(consts_ready, 1)
            g.memset(ln_eps, 4 * LN_EPS).then_inc(consts_ready, 1)
            pool.wait_ge(consts_ready, 6)
            g.affine_select(out=ident, in_=ident, compare_op=ALU.not_equal, fill=1.0, base=0,
                            pattern=[[-1, P]], channel_multiplier=1).then_inc(consts_ready, 1)
            g.affine_select(out=causal[:, P:2 * P], in_=causal[:, P:2 * P], compare_op=ALU.is_ge, fill=MASKED,
                            base=0, pattern=[[-1, P]], channel_multiplier=1).then_inc(consts_ready, 1)

            def inverse_rms(l, n, which, k, t):
                row = t if which == "x" else T + t
                i = 2 * SQUARES.index((which, k, t))
                pool.wait_ge(ss_ready, nth(l, 16, i))
                g.tensor_tensor(ms[:, row, 0:1], ss[:, row, 0:1], norm_eps[:, 0:1], ALU.add).then_inc(ms_ready, 1)
                pool.wait_ge(ms_ready, nth(l, 16, 2 * n))
                pool.wait_ge(ss_ready, nth(l, 16, i + 1))
                g.tensor_tensor(ms[:, row, 1:2], ms[:, row, 0:1], ss[:, row, 1:2], ALU.add).then_inc(ms_ready, 1)
                pool.wait_ge(ms_ready, nth(l, 16, 2 * n + 1))
                g.tensor_tensor(rstd[:, row:row + 1], ms[:, row, 1:2], minus_half[:, 0:1], ALU.pow
                                ).then_inc(rstd_ready, 1)

            with pool.Fori(0, L) as l:
                for n in range(2):
                    inverse_rms(l, n, *SQUARES[n])
                pool.wait_ge(side_landed, 16 * nth(l, 14, 13))
                apart(pool)
                g.affine_select(out=w_s, in_=w_s, compare_op=ALU.is_ge, fill=0.0, base=0,
                                pattern=[[0, A_GROUPS], [-1, P]], channel_multiplier=1).then_inc(ws_masked, 1)
                pool.wait_ge(ln_mv_ready, nth(l, 2, 1))
                g.tensor_tensor(ln_ms, ln_mv[:, :, 1], ln_eps, ALU.add).then_inc(ln_ms_ready, 1)
                pool.wait_ge(ln_ms_ready, nth(l, 1, 0))
                g.tensor_tensor(ln_rstd, ln_ms, minus_half[:, 0:T], ALU.pow).then_inc(ln_rstd_ready, 1)
                pool.wait_ge(ssD_ready, nth(l, 4, 3))
                g.tensor_tensor(msD.rearrange("p n t -> p (n t)"), ssD.rearrange("p n t -> p (n t)"), norm_eps,
                                ALU.add).then_inc(msD_ready, 1)
                pool.wait_ge(msD_ready, nth(l, 1, 0))
                g.tensor_tensor(rstdD.rearrange("p n t -> p (n t)"), msD.rearrange("p n t -> p (n t)"),
                                minus_half, ALU.pow).then_inc(rstdD_ready, 1)
                for i in range(1, NB):
                    for u in range(4):
                        pool.wait_ge(unit_gated, nth(l, 16, 4 * i + u))
                        if i > 1:
                            pool.wait_ge(unit_added, nth(l, 12, 4 * (i - 2) + u))
                        g.tensor_tensor(merged[:, u, :], merged[:, u, :], gated[:, u, :], ALU.add
                                        ).then_inc(unit_added, 1)
                for n in range(2, 8):
                    inverse_rms(l, n, *SQUARES[n])

        @block.tensor
        def _(pe):
            def product(dst, lhs, rhs, first, last):
                (l_hi, l_lo), (r_hi, r_lo) = lhs, rhs
                nc.tensor.matmul(dst, l_hi, r_hi, start=first, stop=False)
                nc.tensor.matmul(dst, l_hi, r_lo, start=False, stop=False)
                return nc.tensor.matmul(dst, l_lo, r_hi, start=False, stop=last)

            def wait_chunk(l, c, i=0):
                pe.wait_ge(lo_ready, split_done(l, c + 4 * i))

            def transpose_x(l, k, t):
                for b in range(2):
                    pe.wait_ge(xn_ready, nth(l, 8, row_half(k, t, b)))
                    for j in range(4):
                        kt = 4 * b + j
                        last = nc.tensor.transpose(psum[:, 4 + 2 * t + b, j * P:(j + 1) * P],
                                                   xn[:, t, kt * P:(kt + 1) * P], ident)
                    last.then_inc(xT_psum, 1)

            def xT(kt, cut=slice(0, S)):
                return xT_hi[:, kt, cut], xT_lo[:, kt, cut]

            def tokens(t):
                return slice(t * P, (t + 1) * P)

            def feature_major(l, c, bank, f=None):
                hi, lo = both(c)
                for f in range(2) if f is None else (f,):
                    cut = slice(f * P, (f + 1) * P)
                    for kt in range(KT):
                        last = product(psum[:, bank, f * S:(f + 1) * S], (hi[:, kt, cut], lo[:, kt, cut]), xT(kt),
                                       kt == 0, kt == KT - 1)
                return last

            def hidden_transposes(l, t):
                pe.wait_ge(hidden_copied, nth(l, 2, t))
                for k in range(2):
                    for f in range(2):
                        last = nc.tensor.transpose(psum[:, 1 + 2 * k, f * S + t * P:f * S + (t + 1) * P],
                                                   hidden_rows[:, t, k * FFC + f * P:k * FFC + (f + 1) * P], ident)
                    if t == 1:
                        last.then_inc(hiddenT_psum, 1)

            def head_scores(l, h):
                n = h % 4
                if h < 4:
                    part = slice(64 * (n % 2), 64 * (n % 2) + 64)
                    q, k = qTB[part, n // 2, :], kTB[part, n // 2, :]
                else:
                    q, k = qTD[0:QK, n, :], kTD[0:QK, n, :]
                if h == 0:
                    pe.wait_ge(qkTB_copied, nth(l, 2, 1))
                    pe.wait_ge(c_out_ready, nth(l, 1, 0))
                if h == 4:
                    pe.wait_ge(qkTD_copied, nth(l, 4, 3))
                if h >= 2:
                    pe.wait_ge(scores_masked, nth(l, 16, 2 * (h - 2) + 1))
                nc.tensor.matmul(psum[:, h % 2, 0:P], q[:, 0:P], k[:, 0:P], start=True, stop=True)
                nc.tensor.matmul(psum[:, h % 2, P:3 * P], q[:, P:S], k, start=True, stop=True
                                 ).then_inc(scores_psum, 1)

            def head_transpose(l, h):
                pe.wait_ge(probs_ready, nth(l, 16, 2 * h + 1))
                if h >= 1:
                    pe.wait_ge(probsT_copied, nth(l, 8, h - 1))
                for b in range(3):
                    last = nc.tensor.transpose(psum[:, 2, b * P:(b + 1) * P], probs[:, h % 2, b * P:(b + 1) * P],
                                               ident)
                last.then_inc(probsT_psum, 1)

            def head_values(l, h):
                pe.wait_ge(probsT_copied, nth(l, 8, h))
                if h == 0:
                    pe.wait_ge(u_gelu, nth(l, 1, 0))
                if h == 4:
                    pe.wait_ge(qkTD_copied, nth(l, 4, 3))
                n = h % 4
                v = [proj[:, t, 3 * MIX + HD * n:3 * MIX + HD * n + HD] if h < 4 else
                     vD[:, t, D_V * n:D_V * n + D_V] for t in range(T)]
                bank, pT = psum[:, (3, 5)[h // 4], :], probsT[:, h % 2, :]
                nc.tensor.matmul(bank[:, HD * n:HD * n + HD], pT[:, 0:P], v[0], start=True, stop=True)
                o = MIX + HD * n
                nc.tensor.matmul(bank[:, o:o + HD], pT[:, P:2 * P], v[0], start=True, stop=False)
                nc.tensor.matmul(bank[:, o:o + HD], pT[:, 2 * P:3 * P], v[1], start=False, stop=True
                                 ).then_inc(attn_psum, 1)

            def side_after(l, c):
                if c == 3:
                    pe.wait_ge(side_landed, 16 * nth(l, 14, 13))
                    apart(pe)
                    nc.tensor.transpose(psum[:, 6, 0:9], vec_rows, ident[0:9, 0:9]).then_inc(vec_psum, 1)
                    pe.wait_ge(ws_masked, nth(l, 1, 0))
                    for g in range(A_GROUPS):
                        last = nc.tensor.transpose(psum[:, 7, g * P:(g + 1) * P], w_s[:, g, :], ident)
                    last.then_inc(wsT_psum, 1)
                if c == 5:
                    pe.wait_ge(ropeB_ready, nth(l, 1, 0))
                    pe.wait_ge(wsT_copied, nth(l, 1, 0))
                    for n in range(2):
                        for f in range(FT):
                            for t in range(T):
                                o = MIX * (1 + n) + f * P
                                last = nc.tensor.transpose(psum[:, 6 + n, f * S + t * P:f * S + (t + 1) * P],
                                                           proj[:, t, o:o + P], ident)
                        last.then_inc(qkTB_psum, 1)
                if c == 9:
                    pe.wait_ge(d_normed, nth(l, 1, 0))
                    pe.wait_ge(ssD_ready, nth(l, 4, 3))
                    for t in range(T):
                        nc.tensor.transpose(psum[:, 4, t * P:(t + 1) * P], d_in[:, t, 0:P], ident)
                        nc.tensor.transpose(psum[:, 4, S + t * P:S + (t + 1) * P],
                                            d_in[:, t, Q_LORA:Q_LORA + KV_LORA], ident)
                        last = nc.tensor.transpose(psum[0:Q_LORA - P, 5, t * P:(t + 1) * P],
                                                   d_in[:, t, P:Q_LORA], ident)
                    last.then_inc(d_latentT_psum, 1)
                if c == 10:
                    pe.wait_ge(d_latentT_copied, nth(l, 1, 0))
                    pe.wait_ge(qkTB_copied, nth(l, 2, 1))
                    rest = slice(0, Q_LORA - P)
                    for t in range(T):
                        dst = psum[:, 4 + t, 0:HEADS * QK]
                        nc.tensor.matmul(dst, cqT[:, 0, tokens(t)], w_uq[:, 0, :], start=True, stop=False)
                        nc.tensor.matmul(dst, cqT[rest, 1, tokens(t)], w_uq[rest, 1, :], start=False, stop=True
                                         ).then_inc(qD_psum, 1)
                    for t in range(T):
                        nc.tensor.matmul(psum[:, 6 + t, :], ckvT[:, tokens(t)], w_ukv, start=True, stop=True
                                         ).then_inc(kvD_psum, 1)
                if c in (12, 13):
                    n = c - 12
                    pe.wait_ge(ropeD_ready, nth(l, 2, n))
                    pe.wait_ge(qkvD_copied, nth(l, 1, 0))
                    if n == 1:
                        pe.wait_ge(qkTD_copied, nth(l, 4, 1))
                    src = (qD, kD)[n]
                    for b in range(2):
                        for j in range(2):
                            for t in range(T):
                                last = nc.tensor.transpose(psum[0:QK, 4 + b, j * S + t * P:j * S + (t + 1) * P],
                                                           src[:, t, 2 * b + j, :], ident)
                        last.then_inc(qkTD_psum, 1)
                if c == 14:
                    pe.wait_ge(ln_ready, nth(l, 1, 0))
                    pe.wait_ge(qkTD_copied, nth(l, 4, 3))
                    for g in range(A_GROUPS):
                        part = slice(64 * (g % 2), 64 * (g % 2) + 64)
                        for t in range(T):
                            o = (g // 2) * S + t * P
                            last = nc.tensor.matmul(psum[part, 4, o:o + P], av2[:, t, 64 * g:64 * g + 64],
                                                    w_sT[:, g, :], start=True, stop=True)
                    last.then_inc(sv_psum, 1)
                if 13 <= c < 21:
                    head_scores(l, c - 13)
                if 14 <= c < 22:
                    head_transpose(l, c - 14)
                if 15 <= c < 23:
                    head_values(l, c - 15)
                if c in (19, 23):
                    n = (c - 19) // 4
                    pe.wait_ge(attn_ready, nth(l, 2, n))
                    if n == 0:
                        pe.wait_ge(a_out_ready, nth(l, 1, 0))
                    else:
                        pe.wait_ge(brT_lo_ready, nth(l, 4, ORDER_B))
                    for f in range(FT):
                        for t in range(T):
                            last = nc.tensor.transpose(psum[:, 4, f * S + t * P:f * S + (t + 1) * P],
                                                       o_sb[:, t, f * P:(f + 1) * P], ident)
                    last.then_inc(attnT_psum, 1)

            pe.wait_ge(consts_ready, CONSTS)
            with pe.Fori(0, L) as l:
                for t in range(T):
                    transpose_x(l, 0, t)
                for g in range(2):
                    for t in range(T):
                        for kh in range(2):
                            c = 2 * g + kh
                            wait_chunk(l, c)
                            if g == 0:
                                pe.wait_ge(xT_lo_ready, nth(l, 8, row_half(0, t, kh)))
                            hi, lo = both(c)
                            for j in range(4):
                                kt = 4 * kh + j
                                last = product(psum[:, 2 * t + g, :], xT(kt, tokens(t)), (hi[:, j, :], lo[:, j, :]),
                                               kt == 0, kt == KT - 1)
                            if t == 1:
                                last.then_inc(chunk_used, 1)
                            elif kh == 1:
                                last.then_inc(proj0_psum, 1)
                side_after(l, 3)
                for c in range(C_D, C_FEAT):
                    wait_chunk(l, c)
                    hi, lo = both(c)
                    for t in range(T):
                        for j in range(2):
                            kt = 2 * (c - C_D) + j
                            last = product(psum[:, 4 + t, 0:D_IN], xT(kt, tokens(t)), (hi[:, j, :], lo[:, j, :]),
                                           kt == 0, kt == KT - 1)
                    last.then_inc(chunk_used, 1)
                    side_after(l, c)
                pe.wait_ge(proj_copied, nth(l, 4, 3))
                for c in range(C_FEAT, C_GATE):
                    wait_chunk(l, c)
                    feature_major(l, c, c - C_FEAT).then_inc(chunk_used, 1)
                    side_after(l, c)
                pe.wait_ge(qkvD_copied, nth(l, 1, 0))
                for c in range(C_GATE, C_BRANCH):
                    n = c - C_GATE
                    wait_chunk(l, c)
                    if n >= 2:
                        pe.wait_ge(gate_ready, nth(l, 16, n - 2))
                    feature_major(l, c, 6 + n % 2).then_inc(chunk_used, 1)
                    side_after(l, c)
                for i in range(NB):
                    c = C_BRANCH + i
                    wait_chunk(l, c)
                    if i == 0:
                        pe.wait_ge(brT_lo_ready, nth(l, 4, ORDER_D))
                        pe.wait_ge(gate_ready, nth(l, 16, 15))
                    hi, lo = both(c)
                    for u in range(4):
                        if i >= 1:
                            pe.wait_ge(unit_gated, nth(l, 16, 4 * (i - 1) + u))
                        for f in range(2):
                            cut = slice((2 * u + f) * P, (2 * u + f + 1) * P)
                            for kt in range(FT):
                                last = product(psum[:, 4 + u, f * S:(f + 1) * S], (hi[:, kt, cut], lo[:, kt, cut]),
                                               (brT_hi[:, FT * i + kt, :], brT_lo[:, FT * i + kt, :]),
                                               kt == 0, kt == FT - 1)
                        last.then_inc(unit_psum if u < 3 else chunk_used, 1)
                def output(l, c, t, h):
                    hi, lo = both(c)
                    for j in range(2):
                        kt = 2 * (c - C_OUT) + j
                        last = product(psum[:, 2 * t + h, :], xT(kt, tokens(t)),
                                       (hi[:, j, columns(h)], lo[:, j, columns(h)]), kt == 0, kt == KT - 1)
                    return last

                for h in range(2):
                    for c in range(C_OUT, C_MLP - 1):
                        if h == 0:
                            wait_chunk(l, c)
                            pe.wait_ge(mergedT_lo_ready, nth(l, 4, c - C_OUT))
                        output(l, c, 0, h)
                wait_chunk(l, C_MLP - 1)
                pe.wait_ge(mergedT_lo_ready, nth(l, 4, 3))
                for h in range(2):
                    output(l, C_MLP - 1, 0, h).then_inc(y_psum, 1)
                for c in range(C_OUT, C_MLP):
                    if c == C_MLP - 1:
                        transpose_x(l, 1, 0)
                    for h in range(2):
                        last = output(l, c, 1, h)
                        if c == C_MLP - 1 and h == 0:
                            last.then_inc(y_psum, 1)
                    last.then_inc(chunk_used, 1)

                for t in range(T):
                    if t == 1:
                        transpose_x(l, 1, 1)
                        hidden_transposes(l, 0)
                    for k in range(2):
                        wait_chunk(l, C_MLP + k)
                        hi, lo = both(C_MLP + k)
                        for kt in range(KT):
                            if k == 0 and kt % 4 == 0:
                                pe.wait_ge(xT_lo_ready, nth(l, 8, row_half(1, t, kt // 4)))
                            last = product(psum[:, 2 * t, k * FFC:(k + 1) * FFC], xT(kt, tokens(t)),
                                           (hi[:, kt, :], lo[:, kt, :]), kt == 0, kt == KT - 1)
                        if t == 1:
                            last.then_inc(chunk_used, 1)
                    if t == 0:
                        last.then_inc(hidden0_psum, 1)

                def mlp_in(k, c, i=0, f=None):
                    wait_chunk(l, c, i)
                    return feature_major(l, c, 4 + k % 2, f)

                def mlp_out(k, c, i=0, first=False, last=False):
                    wait_chunk(l, c, i)
                    pe.wait_ge(hidden_lo_ready, nth(l, STEPS, k + 2 * i))
                    if first:
                        pe.wait_ge(relu_ready, nth(l, STEPS, 1))
                    hi, lo = both(c)
                    for t in range(T):
                        for h in range(2):
                            for j in range(2):
                                n = 2 * (k % 2) + j
                                mm = product(psum[:, 2 * t + h, :],
                                             (brT_hi[:, n, tokens(t)], brT_lo[:, n, tokens(t)]),
                                             (hi[:, j, columns(h)], lo[:, j, columns(h)]),
                                             first and j == 0, last and j == 1)
                            if t == 1 and h == 1:
                                mm.then_inc(chunk_used, 1)
                            elif last:
                                mm.then_inc(y_psum, 1)

                mlp_in(2, C_IN2, f=0)
                hidden_transposes(l, 1)
                mlp_in(2, C_IN2, f=1).then_inc(chunk_used, 1)
                mlp_out(0, C_LOOP - 1, first=True)
                with pe.Fori(0, PAIRS) as i:
                    for b in range(2):
                        pe.wait_ge(relu_ready, nth(l, STEPS, 1 + b + 2 * i))
                        mlp_in(3 + b, C_LOOP + 2 * b, i).then_inc(chunk_used, 1)
                        mlp_out(1 + b, C_LOOP + 2 * b + 1, i)
                pe.wait_ge(relu_ready, nth(l, STEPS, STEPS - 3))
                mlp_in(STEPS - 1, CHUNKS - 4).then_inc(chunk_used, 1)
                for k in range(STEPS - 3, STEPS):
                    mlp_out(k, CHUNKS - STEPS + k, last=k == STEPS - 1)


_INS = ['x', 'g_pre_mix', 'w_in', 'a_ln_g', 'a_ln_b', 'a_w_s', 'a_b_s', 'c_w_conv', 'd_q_norm_g', 'd_w_uq',
        'd_kv_norm_g', 'd_w_ukv', 'w_branch', 'w_out', 'g_post_mix', 'g_pre_mlp', 'w_mlp_in', 'w_mlp_out',
        'g_post_mlp']
ROPE_THETA = 500000.0


def _rope_tables(seq):
    import numpy as np
    parts = []
    for dim in (B_ROT, D_ROPE):
        exponent = np.arange(0, dim, 2, dtype=np.float32) / np.float32(dim)
        inv = np.float32(1.0) / np.power(np.float64(ROPE_THETA), exponent).astype(np.float32)
        angle = np.arange(seq, dtype=np.float32)[:, None] * inv[None, :]
        parts += [np.cos(angle.astype(np.float64)), np.sin(angle.astype(np.float64))]
    return np.concatenate(parts, axis=1).astype(np.float32)


def kernel(**inputs):
    import numpy as _np
    import concourse.bacc as _bacc
    from concourse import mybir as _mybir
    from concourse.bass_utils import run_bass_kernel_spmd as _run

    nc = _bacc.Bacc("TRN2", target_bir_lowering=False, num_devices=1)
    arrays, args = {}, []
    shape = _np.shape(inputs['x'])
    for name, a in [(n, inputs[n]) for n in _INS] + [('rope_tables', _rope_tables(shape[1]))]:
        a = _np.ascontiguousarray(a)
        arrays[f"in_{name}_dram"] = a
        args.append(nc.dram_tensor(f"in_{name}_dram", a.shape, _mybir.dt.from_np(a.dtype), kind="ExternalInput").ap())
    args.append(nc.dram_tensor("out_0_dram", shape, F32, kind="ExternalOutput").ap())
    hybrid_trunk(nc, *args)
    r = _run(nc, [arrays], core_ids=[0])
    return r.results[0]["out_0_dram"]
```
